# Optimizing a Trainium2 kernel written in Bass

```python
import jax
import jax.numpy as jnp
from jax import lax
import numpy as np

D_MODEL = 1024
BATCH = 1
SEQ = 512
DEPTH = 2

HEAD_DIM = 64
N_HEADS_A = 8
N_HEADS_B = 8
WIDTH_A = N_HEADS_A * HEAD_DIM
WIDTH_B = N_HEADS_B * HEAD_DIM
DILATED_CONFIGS = ((128, 1), (512, 4), (2048, 16))
SEG = 128
Q_BLOCK = 128
RET_HEADS = 4
RET_QK_DIM = D_MODEL // RET_HEADS
RET_V_DIM = 2 * D_MODEL // RET_HEADS
RET_CHUNK = 128
MLP_HIDDEN = 4 * D_MODEL
RMS_EPS = 1e-6
GN_EPS = 1e-6
EVEN_IN = 3 * WIDTH_A + 3 * WIDTH_B + N_HEADS_B
ODD_IN = 6 * D_MODEL
N_EVEN = (DEPTH + 1) // 2
N_ODD = DEPTH // 2

kernel_name = "hybrid_dilated_fox_retention_trunk"

def _rms_norm(x, g):
    xf = x.astype(jnp.float32)
    y = xf * lax.rsqrt(jnp.mean(xf * xf, axis=-1, keepdims=True) + RMS_EPS)
    return (y * g.astype(jnp.float32)).astype(x.dtype)

def _split_heads(t, n):
    b, s, _ = t.shape
    return t.reshape(b, s, n, -1).transpose(0, 2, 1, 3)

def _merge_heads(t):
    b, h, s, e = t.shape
    return t.transpose(0, 2, 1, 3).reshape(b, s, h * e)

def _alibi_slopes(n):
    return 2.0 ** (-8.0 * (jnp.arange(n, dtype=jnp.float32) + 1.0) / n)

def _retention_gammas(n):
    return 1.0 - 2.0 ** (-5.0 - jnp.arange(n, dtype=jnp.float32))

def _to_streams(t, dilation, padded_len):
    b, h, s, e = t.shape
    t = jnp.pad(t, ((0, 0), (0, 0), (0, padded_len - s), (0, 0)))
    t = t.reshape(b, h, padded_len // dilation, dilation, e)
    t = jnp.swapaxes(t, 2, 3)
    return t.reshape(b, h, dilation, padded_len // (dilation * SEG), SEG, e)

def _from_streams(t, s):
    b, h, d, n, _, e = t.shape
    t = t.reshape(b, h, d, n * SEG, e)
    t = jnp.swapaxes(t, 2, 3).reshape(b, h, d * n * SEG, e)
    return t[:, :, :s]

def _dilated_branch(q, k, v, slopes, window, dilation):
    b, h, s, dh = q.shape
    n_steps = window // dilation
    span = dilation * SEG
    padded = -(-s // span) * span
    qs = _to_streams(q, dilation, padded)
    ks = _to_streams(k, dilation, padded)
    vs = _to_streams(v, dilation, padded)
    n_blk = qs.shape[3]
    prev_pad = ((0, 0), (0, 0), (0, 0), (1, 0), (0, 0), (0, 0))
    kk = jnp.concatenate([jnp.pad(ks, prev_pad)[:, :, :, :-1], ks], axis=4)
    vv = jnp.concatenate([jnp.pad(vs, prev_pad)[:, :, :, :-1], vs], axis=4)
    scores = jnp.einsum("bhrnqe,bhrnke->bhrnqk", qs, kk,
                        preferred_element_type=jnp.float32) * (dh ** -0.5)
    qi = jnp.arange(SEG)[:, None]
    ki = jnp.arange(2 * SEG)[None, :]
    steps = qi + SEG - ki
    band = (steps >= 0) & (steps <= n_steps)
    has_prev = (jnp.arange(n_blk) > 0)[:, None, None] | (ki >= SEG)[None]
    valid = band[None] & has_prev
    dist = (steps * dilation).astype(jnp.float32)
    logits = scores - slopes[None, :, None, None, None, None] * dist
    logits = jnp.where(valid, logits, -jnp.inf)
    m = jnp.max(logits, axis=-1, keepdims=True)
    p = jnp.exp(logits - m)
    den = jnp.sum(p, axis=-1, keepdims=True)
    o = jnp.einsum("bhrnqk,bhrnke->bhrnqe", p, vv.astype(jnp.float32)) / den
    lse = m + jnp.log(den)
    return _from_streams(o, s), _from_streams(lse, s)[..., 0]

def _dilated_attention(q, k, v, slopes):
    outs, lses = [], []
    for window, dilation in DILATED_CONFIGS:
        o, l = _dilated_branch(q, k, v, slopes, window, dilation)
        outs.append(o)
        lses.append(l)
    w = jax.nn.softmax(jnp.stack(lses, axis=0), axis=0)
    return jnp.einsum("gbhs,gbhse->bhse", w, jnp.stack(outs, axis=0))

def _forgetting_attention(q, k, v, log_f):
    b, h, s, dh = q.shape
    c = jnp.cumsum(log_f, axis=-1)
    nb = s // Q_BLOCK
    qb = q.reshape(b, h, nb, Q_BLOCK, dh).transpose(2, 0, 1, 3, 4)
    cb = c.reshape(b, h, nb, Q_BLOCK).transpose(2, 0, 1, 3)
    kpos = jnp.arange(s)
    vf = v.astype(jnp.float32)

    def block(args):
        i, q_i, c_i = args
        sc = jnp.einsum("bhqe,bhke->bhqk", q_i, k,
                        preferred_element_type=jnp.float32) * (dh ** -0.5)
        sc = sc + c_i[..., None] - c[:, :, None, :]
        qpos = i * Q_BLOCK + jnp.arange(Q_BLOCK)
        sc = jnp.where(kpos[None, :] <= qpos[:, None], sc, -jnp.inf)
        p = jax.nn.softmax(sc, axis=-1)
        return jnp.einsum("bhqk,bhke->bhqe", p, vf)

    o = lax.map(block, (jnp.arange(nb), qb, cb))
    return o.transpose(1, 2, 0, 3, 4).reshape(b, h, s, dh)

def _retention(q, k, v, gammas):
    b, h, s, dk = q.shape
    dv = v.shape[-1]
    C = RET_CHUNK
    n = s // C
    q = q.astype(jnp.float32)
    k = k.astype(jnp.float32) * (dk ** -0.5)
    v = v.astype(jnp.float32)
    log_g = jnp.log(gammas)
    idx = jnp.arange(C, dtype=jnp.float32)
    rel = idx[:, None] - idx[None, :]
    decay_in = jnp.where(rel >= 0, jnp.exp(log_g[:, None, None] * jnp.maximum(rel, 0.0)), 0.0)
    q_dec = jnp.exp(log_g[:, None] * (idx + 1.0))[None, :, :, None]
    k_dec = jnp.exp(log_g[:, None] * (C - 1.0 - idx))[None, :, :, None]
    chunk_dec = jnp.exp(log_g * C)[None, :, None, None]

    def chunks(t):
        return t.reshape(b, h, n, C, t.shape[-1]).transpose(2, 0, 1, 3, 4)

    def step(state, inp):
        q_i, k_i, v_i = inp
        inner = jnp.einsum("bhqd,bhkd->bhqk", q_i, k_i) * decay_in
        o = (jnp.einsum("bhqk,bhkv->bhqv", inner, v_i)
             + jnp.einsum("bhqd,bhdv->bhqv", q_i, state) * q_dec)
        state = chunk_dec * state + jnp.einsum("bhkd,bhkv->bhdv", k_i * k_dec, v_i)
        return state, o

    state0 = jnp.zeros((b, h, dk, dv), jnp.float32)
    _, o = lax.scan(step, state0, (chunks(q), chunks(k), chunks(v)))
    return o.transpose(1, 2, 0, 3, 4).reshape(b, h, s, dv)

def _even_mixer(h, w_in, b_f, w_out, slopes):
    proj = h @ w_in
    cuts = [WIDTH_A, 2 * WIDTH_A, 3 * WIDTH_A,
            3 * WIDTH_A + WIDTH_B, 3 * WIDTH_A + 2 * WIDTH_B, 3 * WIDTH_A + 3 * WIDTH_B]
    qa, ka, va, qb, kb, vb, f_logit = jnp.split(proj, cuts, axis=-1)
    oa = _dilated_attention(_split_heads(qa, N_HEADS_A), _split_heads(ka, N_HEADS_A),
                            _split_heads(va, N_HEADS_A), slopes)
    log_f = jax.nn.log_sigmoid(f_logit.astype(jnp.float32) + b_f.astype(jnp.float32))
    ob = _forgetting_attention(_split_heads(qb, N_HEADS_B), _split_heads(kb, N_HEADS_B),
                               _split_heads(vb, N_HEADS_B), jnp.swapaxes(log_f, 1, 2))
    o = jnp.concatenate([_merge_heads(oa), _merge_heads(ob)], axis=-1).astype(h.dtype)
    return o @ w_out

def _odd_mixer(h, w_in, w_out, gammas):
    proj = h @ w_in
    q, k, v, g = jnp.split(proj, [D_MODEL, 2 * D_MODEL, 4 * D_MODEL], axis=-1)
    o = _retention(_split_heads(q, RET_HEADS), _split_heads(k, RET_HEADS),
                   _split_heads(v, RET_HEADS), gammas)
    mu = jnp.mean(o, axis=-1, keepdims=True)
    var = jnp.mean(jnp.square(o - mu), axis=-1, keepdims=True)
    o = _merge_heads((o - mu) * lax.rsqrt(var + GN_EPS))
    y = (jax.nn.silu(g.astype(jnp.float32)) * o).astype(h.dtype)
    return y @ w_out

def _squared_relu_mlp(h, w1, w2):
    return jnp.square(jax.nn.relu(h @ w1)) @ w2

def setup_inputs(seed: int = 0) -> dict:
    key = jax.random.key(seed)
    ks = jax.random.split(key, 12)
    f32 = jnp.float32
    out_scale = (2.0 * DEPTH) ** -0.5

    def dense(k, shape, fan_in, scale=1.0):
        return jax.random.normal(k, shape, f32) * (scale * fan_in ** -0.5)

    return {
        "x": jax.random.normal(ks[0], (BATCH, SEQ, D_MODEL), f32),
        "norm_mix_g": 1.0 + 0.02 * jax.random.normal(ks[1], (DEPTH, D_MODEL), f32),
        "norm_ffn_g": 1.0 + 0.02 * jax.random.normal(ks[2], (DEPTH, D_MODEL), f32),
        "even_w_in": dense(ks[3], (N_EVEN, D_MODEL, EVEN_IN), D_MODEL),
        "even_b_f": 2.0 + 0.5 * jax.random.normal(ks[4], (N_EVEN, N_HEADS_B), f32),
        "even_w_out": dense(ks[5], (N_EVEN, WIDTH_A + WIDTH_B, D_MODEL), WIDTH_A + WIDTH_B, out_scale),
        "odd_w_in": dense(ks[6], (N_ODD, D_MODEL, ODD_IN), D_MODEL),
        "odd_w_out": dense(ks[7], (N_ODD, 2 * D_MODEL, D_MODEL), 2 * D_MODEL, out_scale),
        "ffn_w_in": dense(ks[8], (DEPTH, D_MODEL, MLP_HIDDEN), D_MODEL),
        "ffn_w_out": dense(ks[9], (DEPTH, MLP_HIDDEN, D_MODEL), MLP_HIDDEN, out_scale),
        "final_g": 1.0 + 0.02 * jax.random.normal(ks[10], (D_MODEL,), f32),
    }

def reference(x, norm_mix_g, norm_ffn_g, even_w_in, even_b_f, even_w_out,
              odd_w_in, odd_w_out, ffn_w_in, ffn_w_out, final_g):
    slopes = _alibi_slopes(N_HEADS_A)
    gammas = _retention_gammas(RET_HEADS)
    for layer in range(DEPTH):
        h = _rms_norm(x, norm_mix_g[layer])
        if layer % 2 == 0:
            i = layer // 2
            x = x + _even_mixer(h, even_w_in[i], even_b_f[i], even_w_out[i], slopes)
        else:
            i = layer // 2
            x = x + _odd_mixer(h, odd_w_in[i], odd_w_out[i], gammas)
        h = _rms_norm(x, norm_ffn_g[layer])
        x = x + _squared_relu_mlp(h, ffn_w_in[layer], ffn_w_out[layer])
    return _rms_norm(x, final_g)


_drawn_inputs = setup_inputs


def setup_inputs(seed=0):
    import zlib

    import numpy as np

    out = dict(_drawn_inputs(seed))
    spreads = {}
    factors = {'norm_mix_g': 3.677, 'norm_ffn_g': 3.289, 'final_g': 2.927}
    for name, (base, spread) in spreads.items():
        noise = np.random.default_rng([zlib.crc32(name.encode()), seed]).standard_normal(out[name].shape)
        drawn = base * np.exp(spread * noise) if base else spread * noise
        out[name] = jnp.asarray(drawn.astype(out[name].dtype))
    for name, factor in factors.items():
        out[name] = (out[name] * factor).astype(out[name].dtype)
    return out
```

```python
from contextlib import ExitStack

import numpy as np

import concourse.bass as bass
from concourse import mybir

F32 = mybir.dt.float32
F32R = mybir.dt.float32r
BF16 = mybir.dt.bfloat16
ALU = mybir.AluOpType
ACT = mybir.ActivationFunctionType

P = 128
S = 512
D = 1024
TT = S // P
KT = D // P
HD = 64
WA = 512
NPAIR = 8
NHEAD = 16
NFOX = 8
RH = 4
RV = 512
HID = 4096
CHUNKS = HID // D
EPS = 1e-6
PASSES = ((0, 0), (0, 1), (1, 0))
NEG = -1e30
BIG = 3.0e38

PAN_E, PAN_M0, PAN_O, PAN_M1, PANELS = 0, 8, 24, 40, 56
JOB_E, JOB_M0, JOB_O, JOB_M1 = 0, 33, 97, 177
AEV_M0, AEV_O, AEV_M1 = 24, 56, 104
DEV_M0, DEV_O, DEV_M1 = 9, 41, 73
DEV_END = 105

E_PANELS = [("v", 0), ("qk", 0), ("qk", 1), ("qk", 2), ("v", 1), ("qk", 3), ("out", 0), ("out", 1)]
GATE_JOB = 4


def first_bank(jobs, q):
    return 2 + q if q < 2 else (jobs + q) % 2


def e_first_job(n):
    return 4 * n + (1 if n >= 1 else 0)


def e_job_of(pair, which):
    panel = {0: 1, 1: 2, 2: 3, 3: 5}[pair // 2]
    return e_first_job(panel) + 2 * (pair % 2) + which


def e_aev(job):
    return job + 1 if job < GATE_JOB else job


STEP_AFTER = {7: [0], 8: [1], 9: [2], 10: [3], 11: [4], 12: [5], 13: [6], 14: [7], 15: [None],
              19: [8], 21: [9], 22: [10], 23: [11], 24: [12, 13, 14, 15, None]}
UNITS = ((3,), (2, 0), (1,))
ORDER = (3, 2, 0, 1)
OFF = {3: 0, 2: 512, 0: 896, 1: 1024}


def attention_steps(job):
    for h in STEP_AFTER.get(job, []):
        if h is None:
            g = 7 if job == 15 else 15
        else:
            g = h - 1 if h not in (0, 8) else None
        t = None
        if h is None:
            t = None
        elif h % 2 == 1 and h >= 3 and h != 9:
            t = (h - 3) // 2
        yield h, g, t


TURN_AFTER_JOB = {16: 3, 24: 7}


def trunk(nc, x_in, norm_mix_g, norm_ffn_g, even_w_in, even_b_f, even_w_out, odd_w_in, odd_w_out,
          ffn_w_in, ffn_w_out, final_g, c_ident, c_causal, c_delta, c_lncount, c_decay, out, negc_dram):
    gains = [norm_mix_g[0:1, :], norm_ffn_g[0:1, :], norm_mix_g[1:2, :], norm_ffn_g[1:2, :],
             final_g.rearrange("(a d) -> a d", a=1)]
    x_tiles = x_in.rearrange("b (t p) d -> (b t) p d", p=P)
    out_tiles = out.rearrange("b (t p) d -> (b t) p d", p=P)
    w_even = even_w_in[0]
    w_eout = even_w_out[0]
    w_odd = odd_w_in[0]
    w_oout = odd_w_out[0]

    with ExitStack() as ctx:
        def sb(name, shape, dt=F32):
            return ctx.enter_context(nc.sbuf_tensor(name, shape, dt))

        def sem(name):
            return ctx.enter_context(nc.semaphore(name))

        slots = [[sb(f"w_{part}{s}", [P, 8, 512], F32R) for part in ("hi", "lo")] for s in range(2)]
        raw = sb("raw", [P, 4, 2, 512])
        x = sb("x", [P, TT, D])
        hT = [sb(f"hT_{part}", [P, KT, S], F32R) for part in ("hi", "lo")]
        gain = sb("gain", [P, D])
        arena = sb("arena", [P, 10496])
        arena_r = sb("arena_r", [P, 16, S], F32R)
        ident = sb("ident", [P, P])
        ident_bf = sb("ident_bf", [P, P], BF16)
        causal_bf = sb("causal_bf", [P, P], BF16)
        wf = sb("wf", [P, KT, NFOX])
        wf_split = [sb(f"wf_{part}", [P, KT, NFOX], F32R) for part in ("hi", "lo")]
        bias_f = sb("bias_f", [NFOX, 1])
        negmax = sb("negmax", [P, 2, 4])
        den = sb("den", [P, 2, 8])
        rden = sb("rden", [P, 8])
        ssum = sb("ssum", [P, 4])
        var = sb("var", [P, 4])
        rstd = sb("rstd", [P, 4])
        half_neg = sb("half_neg", [P, 1])
        gn_stats = sb("gn_stats", [P, 4, 6])
        gn_mv = sb("gn_mv", [P, 4, 2])
        gn_var = sb("gn_var", [P, 4])
        gn_rstd = sb("gn_rstd", [P, 4])

        v_sb = arena[:, 0:2048].rearrange("p (t n) -> p t n", t=TT)
        qk_sb = arena[:, 2048:4096].rearrange("p (s w n) -> p s w n", s=2, w=2)
        prob = arena[:, 4096:6656].rearrange("p (s n) -> p s n", s=2)
        probT = arena[:, 6656:7936]
        table = arena[:, 7936:8960].rearrange("p (s n) -> p s n", s=2)
        delta = arena[:, 8960:9472]
        lncount = arena[:, 9472:9984]
        o_sb = arena[:, 9984:10496]
        gate = arena[0:NFOX, 4096:6144].rearrange("p (s n) -> p s n", s=4)
        negc = o_sb[0:NFOX, :]
        causal = table[:, 0, 0:P]
        xn = arena[:, 4096:6144].rearrange("p (s n) -> p s n", s=2)
        junk = arena[:, 6656:7680]
        relu_sb = arena[:, 0:1024].rearrange("p (s n) -> p s n", s=2)
        sq_sb = arena[:, 1024:2048].rearrange("p (s n) -> p s n", s=2)
        rq_sb = arena[:, 2048:3072].rearrange("p (s n) -> p s n", s=2)
        rk_sb = arena[:, 3072:4096].rearrange("p (s n) -> p s n", s=2)
        att = arena[:, 4096:5376]
        y_sb = arena[:, 6144:8192].rearrange("p (t n) -> p t n", t=TT)
        decay = arena[:, 8192:10240].rearrange("p (h n) -> p h n", h=RH)
        ATT_OFF = (0, 512, 896, 1152)
        oT = [arena_r[:, 0:8, :], arena_r[:, 8:16, :]]
        hid = oT
        yT = [arena_r[:, 0:4, :], arena_r[:, 4:8, :]]

        bank = [ctx.enter_context(nc.psum_tensor(f"bank{i}", [P, 512], F32)) for i in range(8)]

        raw_landed = [sem(f"raw_landed{c}") for c in range(4)]
        hi_split = sem("hi_split")
        lo_split = sem("lo_split")
        job_done = sem("job_done")
        aev = sem("aev")
        dev = sem("dev")
        x_landed = [sem(f"x_landed{t}") for t in range(TT)]
        ident_landed = sem("ident_landed")
        const_landed = sem("const_landed")
        wf_landed = sem("wf_landed")
        gain_landed = sem("gain_landed")
        decay_landed = sem("decay_landed")
        consts_made = sem("consts_made")
        half_made = sem("half_made")
        wf_hi = sem("wf_hi")
        wf_lo = sem("wf_lo")
        ss_ready = sem("ss_ready")
        var_ready = sem("var_ready")
        rstd_ready = sem("rstd_ready")
        xn_ready = sem("xn_ready")
        xnT_done = sem("xnT_done")
        hT_hi = sem("hT_hi")
        hT_lo = sem("hT_lo")
        gate_z = sem("gate_z")
        gate_abs = sem("gate_abs")
        gate_min = sem("gate_min")
        gate_exp = sem("gate_exp")
        gate_ln = sem("gate_ln")
        negc_ready = sem("negc_ready")
        negc_saved = sem("negc_saved")
        table_tmp = sem("table_tmp")
        table_ready = sem("table_ready")
        bias_landed = [sem(f"bias_landed{i}") for i in range(2)]
        score_done = sem("score_done")
        logit_ready = sem("logit_ready")
        prob_ready = sem("prob_ready")
        ptT_done = sem("ptT_done")
        pt_ab = sem("pt_ab")
        pt_c = sem("pt_c")
        pv_done = sem("pv_done")
        rden_ready = sem("rden_ready")
        o_norm = sem("o_norm")
        oT_done = sem("oT_done")
        oT_hi = sem("oT_hi")
        oT_lo = sem("oT_lo")
        sq_ready = sem("sq_ready")
        hid_hi = sem("hid_hi")
        hid_lo = sem("hid_lo")
        rs_done = sem("rs_done")
        att_ready = sem("att_ready")
        ro_done = sem("ro_done")
        gn_st = sem("gn_st")
        gn_ag = sem("gn_ag")
        gn_v = sem("gn_v")
        gn_r = sem("gn_r")
        y_part = sem("y_part")
        y_ready = sem("y_ready")
        yT_done = sem("yT_done")
        yT_hi = sem("yT_hi")
        yT_lo = sem("yT_lo")
        out_saved = [sem(f"out_saved{i}") for i in range(2)]

        block = ctx.enter_context(nc.Block())

        @block.sync
        def _(sp):
            def load_x(t):
                sp.dma_start(x[:, t, :], x_tiles[t]).then_inc(x_landed[t], 16)

            def quarter(n, c, srcs):
                if not (isinstance(n, int) and n == 0):
                    sp.wait_ge(lo_split, 4 * n + c - 3)
                for e, src in enumerate(srcs):
                    dst = raw[:, c, e, :]
                    if len(src.shape) == 3:
                        dst = dst.rearrange("p (w n) -> p w n", w=2)
                    sp.dma_start(dst, src).then_inc(raw_landed[c], 16)

            def plain(w, r0, c0):
                return [w[bass.ds(r0 + P * k, P), bass.ds(c0, 512)] for k in range(KT)]

            def query_key(w, c0, width):
                return [w[P * k:P * k + P, bass.ds(c0, 2 * width)].rearrange("p (w n) -> p w n", w=2)[:, :, 0:256]
                        for k in range(KT)]

            def panel(n, srcs):
                for c in range(4):
                    quarter(n, c, srcs[2 * c:2 * c + 2])

            def e_panel(n):
                kind, i = E_PANELS[n]
                if kind == "v":
                    return plain(w_even, 0, 3 * WA * i + 2 * WA)
                if kind == "qk":
                    return query_key(w_even, 3 * WA * (i // 2) + 256 * (i % 2), WA)
                return plain(w_eout, 0, 512 * i)

            load_x(0)
            sp.dma_start(ident[:, :], c_ident).then_inc(ident_landed, 16)
            first = e_panel(0)
            quarter(0, 0, first[0:2])
            load_x(1)
            for c in range(1, 4):
                quarter(0, c, first[2 * c:2 * c + 2])
            load_x(2)
            load_x(3)
            with nc.allow_non_contiguous_dma(reason="eight biases, one a partition"):
                for dst, src in ((causal, c_causal), (delta, c_delta), (lncount, c_lncount),
                                 (bias_f[:, :], even_b_f.rearrange("a f -> f a"))):
                    sp.dma_start(dst, src).then_inc(const_landed, 16)
            sp.dma_start(wf[:, :, :], w_even[:, 6 * WA:6 * WA + NFOX].rearrange("(k p) n -> p k n", p=P)
                         ).then_inc(wf_landed, 16)
            for n in range(1, PAN_M0):
                panel(n, e_panel(n))

            def mlp(layer, base, c):
                w1, w2 = ffn_w_in[layer], ffn_w_out[layer]
                for e in range(2):
                    panel(base + 4 * c + e, plain(w1, 0, 1024 * c + 512 * e))
                for e in range(2):
                    panel(base + 4 * c + 2 + e, plain(w2, 1024 * c, 512 * e))

            with sp.Fori(0, CHUNKS) as c:
                mlp(0, PAN_M0, c)

            def head_qk(h):
                v = w_odd[:, 0:2 * D].rearrange("r (w n) -> r w n", w=2)
                return [v[P * k:P * k + P, :, bass.ds(256 * h, 256)] for k in range(KT)]

            def head_out(h):
                return [w_oout[bass.ds(512 * h + P * c, P), 512 * f:512 * f + 512] for c in range(4) for f in range(2)]

            panel(PAN_O, head_qk(0))
            panel(PAN_O + 1, plain(w_odd, 0, 2 * D))
            panel(PAN_O + 2, plain(w_odd, 0, 4 * D))
            with sp.Fori(1, RH) as h:
                panel(PAN_O - 1 + 4 * h, head_qk(h))
                panel(PAN_O + 4 * h, head_out(h - 1))
                panel(PAN_O + 1 + 4 * h, plain(w_odd, 0, 2 * D + 512 * h))
                panel(PAN_O + 2 + 4 * h, plain(w_odd, 0, 4 * D + 512 * h))
            panel(PAN_O + 15, head_out(RH - 1))
            with sp.Fori(0, CHUNKS) as c:
                mlp(1, PAN_M1, c)
            for t in range(TT):
                sp.wait_ge(xn_ready, 16 + t + 1)
                sp.dma_start(out_tiles[t], xn[:, t % 2, :]).then_inc(out_saved[t % 2], 16)
            for i in range(2):
                sp.wait_ge(out_saved[i], 16 * TT // 2)

        @block.tensor
        def _(pe):
            def job(parity, stat, mov, slot_waits, kts=KT, first=None):
                for k in range(kts):
                    slot_waits(k)
                    for n, (a, b) in enumerate(PASSES):
                        mm = pe.matmul(bank[parity][:, :] if first is None else bank[parity][0:first, :],
                                       stat(k, a), mov(k, b),
                                       start=(k == 0 and n == 0), stop=(k == kts - 1 and n == 2))
                mm.then_inc(job_done, 1)

            def nowait(k):
                pass

            def quarter_wait(n):
                def w(k):
                    if k % 2 == 0:
                        pe.wait_ge(lo_split, 4 * n + k // 2 + 1)
                return w

            def turn_xn(norm, t):
                pe.wait_ge(xn_ready, 4 * norm + t + 1)
                for b in range(2):
                    if t >= 2:
                        pe.wait_ge(hT_lo, 8 * norm + 2 * (t - 2) + b + 1)
                    dst = bank[4 + 2 * (t % 2) + b]
                    for k in range(4):
                        mm = pe.transpose(dst[:, P * k:P * k + P],
                                          xn[:, t % 2, P * (4 * b + k):P * (4 * b + k) + P], ident[:, :])
                    mm.then_inc(xnT_done, 1)

            def first_panel(norm, n, slot):
                w = slots[slot]
                jobs, devs = {1: (JOB_M0, DEV_M0), 2: (JOB_O, DEV_O), 3: (JOB_M1, DEV_M1)}[norm]
                turn_xn(norm, 2)
                for half in range(2):
                    pe.wait_ge(hT_lo, 8 * norm + 4 * half + 4)
                    for q in range(4):
                        if half == 0 and q == 2:
                            turn_xn(norm, 3)
                            pe.wait_ge(dev, devs)
                        dst = bank[first_bank(jobs, q)]
                        c = 256 * half
                        for k in range(KT):
                            if half == 0 and q == 0 and k % 2 == 0:
                                pe.wait_ge(lo_split, 4 * n + k // 2 + 1)
                            for i, (a, b) in enumerate(PASSES):
                                mm = pe.matmul(dst[:, c:c + 256], w[a][:, k, P * q:P * q + P],
                                               hT[b][:, k, c:c + 256],
                                               start=(k == 0 and i == 0), stop=(k == KT - 1 and i == 2))
                        if half == 1:
                            mm.then_inc(job_done, 1)

            pe.wait_ge(ident_landed, 16)

            def scores_unit(h, u):
                q = 3 * h + u
                ready = ((4 * h - 1), 4 * h, 4 * h + 1)[u]
                if ready > 0:
                    pe.wait_ge(logit_ready, ready)
                if u == 0:
                    pair = h // 2
                    pe.wait_ge(aev, e_aev(e_job_of(pair, 1)))
                dst = bank[2 + q % 2]
                col = 0
                rows = slice(HD * (h % 2), HD * (h % 2) + HD)
                st = (h // 2) % 2
                fox = h >= 8
                if h == 8 and u == 0:
                    pe.wait_ge(consts_made, 2)
                for tb in UNITS[u]:
                    n = P * (tb + 1)
                    mm = pe.matmul(dst[:, col:col + n], qk_sb[rows, st, 0, P * tb:P * tb + P],
                                   qk_sb[rows, st, 1, 0:n], start=True, stop=not fox)
                    if fox:
                        mm = pe.matmul(dst[:, col + n - P:col + n], ident_bf[:, :], causal_bf[:, :],
                                       start=False, stop=True)
                    col += n
                mm.then_inc(score_done, 1)

            def turn_prob(h, u):
                q = 3 * h + u
                pe.wait_ge(prob_ready, 4 * h + (1, 3, 4)[u])
                if u == 0 and h >= 1:
                    pe.wait_ge(pt_ab, 2 * h)
                if u == 1 and h >= 1:
                    pe.wait_ge(pt_c, h)
                if u == 2:
                    pe.wait_ge(pt_ab, 2 * h + 1)
                dst = bank[4 + q % 2]
                col = 0
                for tb in UNITS[u]:
                    for s in range(tb + 1):
                        mm = pe.transpose(dst[:, col:col + P], prob[:, h % 2, OFF[tb] + P * s:OFF[tb] + P * s + P],
                                          ident[:, :])
                        col += P
                mm.then_inc(ptT_done, 1)

            def gather_values(h):
                if h % 2 == 0 and h >= 2:
                    pe.wait_ge(o_norm, h // 2)
                pe.wait_ge(aev, e_aev(e_first_job(0 if h < 8 else 4) + 3))
                for u, need, which in ((0, 2 * h + 1, pt_ab), (1, 2 * h + 2, pt_ab), (2, h + 1, pt_c)):
                    pe.wait_ge(which, need)
                    for tb in UNITS[u]:
                        for s in range(tb + 1):
                            c = P * tb + HD * (h % 2)
                            mm = pe.matmul(bank[6][:, c:c + HD], probT[:, OFF[tb] + P * s:OFF[tb] + P * s + P],
                                           v_sb[:, s, HD * (h % 8):HD * (h % 8) + HD],
                                           start=(s == 0), stop=(s == tb))
                mm.then_inc(pv_done, 1)

            def turn_output(pair):
                pe.wait_ge(o_norm, pair + 1)
                if pair:
                    pe.wait_ge(oT_lo, pair)
                for t in range(TT):
                    mm = pe.transpose(bank[7][:, P * t:P * t + P], o_sb[:, P * t:P * t + P], ident[:, :])
                mm.then_inc(oT_done, 1)

            def attention(j):
                for h, g, pair in attention_steps(j):
                    if pair is not None:
                        turn_output(pair)
                    for u in range(3):
                        if h is not None:
                            scores_unit(h, u)
                        if g is not None:
                            turn_prob(g, u)
                    if g is not None:
                        gather_values(g)
                if j in TURN_AFTER_JOB:
                    turn_output(TURN_AFTER_JOB[j])

            def e_job_free(j):
                if j < 2:
                    return
                p = j - 2
                if p == GATE_JOB:
                    pe.wait_ge(dev, 1)
                elif p < 25:
                    pe.wait_ge(aev, e_aev(p))
                else:
                    pe.wait_ge(dev, 1 + p - 24)

            for n, (kind, i) in enumerate(E_PANELS):
                w = slots[n % 2]
                for q in range(4):
                    j = e_first_job(n) + q
                    if n == 0:
                        for t in ((0, 1), (2,), (3,), ())[q]:
                            turn_xn(0, t)
                        pe.wait_ge(hT_lo, 2 * (q + 1))
                    e_job_free(j)
                    waits = quarter_wait(n) if q == 0 else nowait
                    if kind == "v":
                        job(j % 2, lambda k, a: hT[a][:, k, P * q:P * q + P], lambda k, b: w[b][:, k, :], waits)
                    elif kind == "qk":
                        c = 256 * (q % 2) + P * (q // 2)
                        job(j % 2, lambda k, a: w[a][:, k, c:c + P], lambda k, b: hT[b][:, k, :], waits)
                    else:
                        def both(k, waits=waits, j=j):
                            waits(k)
                            if j == e_first_job(6):
                                pe.wait_ge(oT_lo, k + 1)
                        job(j % 2, lambda k, a: oT[a][:, k, P * q:P * q + P], lambda k, b: w[b][:, k, :], both)
                        if i == 1 and q in (1, 2):
                            turn_xn(1, q - 1)
                    attention(j)
                if n == 0:
                    e_job_free(GATE_JOB)
                    pe.wait_ge(wf_lo, 1)
                    job(GATE_JOB % 2, lambda k, a: wf_split[a][:, k, :], lambda k, b: hT[b][:, k, :], nowait,
                        first=NFOX)

            def mlp(c, pan, jobs, avs, dvs, first=None, last=None):
                if first is not None:
                    first_panel(first, pan, 0)
                for j in range(0 if first is None else 4, 8):
                    w = slots[j // 4]
                    if j < 2:
                        pe.wait_ge(dev, dvs + 8 * c - 1 + j)
                    else:
                        pe.wait_ge(aev, avs + 8 * c + j - 1)
                    waits = quarter_wait(pan + 4 * c + j // 4) if j % 4 == 0 else nowait
                    col = P * (j % 4)
                    job((jobs + j) % 2, lambda k, a: w[a][:, k, col:col + P], lambda k, b: hT[b][:, k, :], waits)
                for q in range(8):
                    w = slots[q // 4]
                    if q < 2:
                        pe.wait_ge(aev, avs + 8 * c + 7 + q)
                    else:
                        pe.wait_ge(dev, dvs + 8 * c + q - 1)
                    waits = quarter_wait(pan + 4 * c + 2 + q // 4) if q % 4 == 0 else nowait

                    def both(k, waits=waits, q=q):
                        waits(k)
                        if q == 0:
                            pe.wait_ge(hid_lo, (avs_hid[jobs]) + 8 * c + k + 1)
                    t = q % 4
                    job((jobs + q) % 2, lambda k, a: hid[a][:, k, P * t:P * t + P], lambda k, b: w[b][:, k, :], both)
                    if last is not None and q in (5, 6):
                        turn_xn(last, q - 5)

            avs_hid = {JOB_M0: 0, JOB_M1: 32}
            mlp(0, PAN_M0, JOB_M0, AEV_M0, DEV_M0, first=1)
            with pe.Fori(1, CHUNKS - 1) as c:
                mlp(c, PAN_M0, JOB_M0, AEV_M0, DEV_M0)
            mlp(CHUNKS - 1, PAN_M0, JOB_M0, AEV_M0, DEV_M0, last=2)


            def r_free(h, stage, q):
                if stage == "qk":
                    if q < 2:
                        pe.wait_ge(aev, AEV_O + 12 * h - 1 + q)
                    else:
                        pe.wait_ge(aev, AEV_O + 12 * h + q - 1)
                elif stage == "out":
                    if q < 2:
                        pe.wait_ge(aev, AEV_O + 12 * h + q + (-1 if isinstance(h, int) else 3))
                    else:
                        pe.wait_ge(dev, DEV_O + 8 * (h - 1) + q - 1)
                elif stage == "v":
                    if q < 2 and not (isinstance(h, int) and h == 0):
                        pe.wait_ge(dev, DEV_O + 8 * (h - 1) + 7 + q)
                    else:
                        pe.wait_ge(aev, AEV_O + 12 * h + 3 + q)
                else:
                    pe.wait_ge(aev, AEV_O + 12 * h + 7 + q)

            def r_qk(h, n, s):
                w = slots[s]
                for q in range(4):
                    r_free(h, "qk", q)
                    job((JOB_O + q) % 2, lambda k, a: w[a][:, k, P * q:P * q + P], lambda k, b: hT[b][:, k, :],
                        quarter_wait(n) if q == 0 else nowait)

            def r_vg(h, n, s, stage):
                w = slots[s]
                for q in range(4):
                    r_free(h, stage, q)
                    job((JOB_O + q) % 2, lambda k, a: hT[a][:, k, P * q:P * q + P], lambda k, b: w[b][:, k, :],
                        quarter_wait(n) if q == 0 else nowait)

            def r_scores(h):
                for s in range(4):
                    if s == 0:
                        pe.wait_ge(aev, AEV_O + 12 * h + 4)
                    if s >= 2:
                        pe.wait_ge(att_ready, 4 * h + s - 1)
                    n = S - P * s
                    for w in range(2):
                        mm = pe.matmul(bank[2 + s % 2][:, 0:n], rk_sb[:, w, P * s:P * s + P],
                                       rq_sb[:, w, P * s:S], start=(w == 0), stop=(w == 1))
                    mm.then_inc(rs_done, 1)

            def r_values(h):
                pe.wait_ge(aev, AEV_O + 12 * h + 8)
                for t in range(4):
                    pe.wait_ge(att_ready, 4 * h + t + 1)
                    for s in range(t + 1):
                        o = ATT_OFF[s] + P * (t - s)
                        mm = pe.matmul(bank[4 + t][:, :], att[:, o:o + P], v_sb[:, s, :],
                                       start=(s == 0), stop=(s == t))
                    mm.then_inc(ro_done, 1)

            def r_turn(h):
                for k in range(4):
                    if k >= 2:
                        pe.wait_ge(yT_lo, 4 * h + k - 1)
                    for t in range(4):
                        if k == 0:
                            pe.wait_ge(y_ready, 4 * h + t + 1)
                        mm = pe.transpose(bank[2 + k % 2][:, P * t:P * t + P], y_sb[:, t, P * k:P * k + P], ident[:, :])
                    mm.then_inc(yT_done, 1)

            def r_out(h, n, s, at):
                w = [slots[s][b][:, :, :].rearrange("p (k f) n -> p k (f n)", f=2) for b in range(2)]
                for q in range(8):
                    r_free(at, "out", q)
                    f, t = q // 4, q % 4

                    def waits(k, q=q):
                        if q == 0:
                            pe.wait_ge(lo_split, 4 * n + k + 1)
                            pe.wait_ge(yT_lo, 4 * h + k + 1)
                    job((JOB_O + q) % 2, lambda k, a: yT[a][:, k, P * t:P * t + P],
                        lambda k, b: w[b][:, k, 512 * f:512 * f + 512], waits, kts=4)
                    if isinstance(at, int) and q in (6, 7):
                        turn_xn(3, q - 6)

            first_panel(2, PAN_O, 0)
            r_vg(0, PAN_O + 1, 1, "v")
            r_scores(0)
            r_vg(0, PAN_O + 2, 0, "g")
            r_values(0)
            with pe.Fori(1, RH) as h:
                r_qk(h, PAN_O - 1 + 4 * h, 1)
                r_turn(h - 1)
                r_out(h - 1, PAN_O + 4 * h, 0, h)
                r_vg(h, PAN_O + 1 + 4 * h, 1, "v")
                r_scores(h)
                r_vg(h, PAN_O + 2 + 4 * h, 0, "g")
                r_values(h)
            r_turn(RH - 1)
            r_out(RH - 1, PAN_O + 15, 1, RH)

            mlp(0, PAN_M1, JOB_M1, AEV_M1, DEV_M1, first=3)
            with pe.Fori(1, CHUNKS) as c:
                mlp(c, PAN_M1, JOB_M1, AEV_M1, DEV_M1)

        @block.scalar
        def _(act):
            def split(n, c, slot, first_job=None):
                if first_job is not None:
                    act.wait_ge(job_done, first_job)
                act.wait_ge(raw_landed[c], 32 * n + 32)
                nc.scalar.activation(slots[slot][0][:, 2 * c:2 * c + 2, :], raw[:, c], ACT.Copy).then_inc(hi_split, 1)

            def square_sum(norm, t):
                if norm == 0:
                    act.wait_ge(x_landed[t], 16)
                else:
                    act.wait_ge(dev, (DEV_M0, DEV_O, DEV_M1, DEV_END)[norm - 1] - 3 + t)
                if norm >= 1 or t >= 1:
                    act.wait_ge(ss_ready, 4 * norm + t)
                nc.scalar.activation(junk, x[:, t, :], ACT.Square, accum_out=ssum[:, t:t + 1]).then_inc(ss_ready, 1)

            def hT_parts(norm, t):
                for b in range(2):
                    act.wait_ge(xnT_done, 8 * norm + 2 * t + b + 1)
                    nc.scalar.activation(hT[0][:, 4 * b:4 * b + 4, P * t:P * t + P],
                                         bank[4 + 2 * (t % 2) + b][:, :].rearrange("p (k n) -> p k n", k=4),
                                         ACT.Copy).then_inc(hT_hi, 1)

            def norm_tiles(norm):
                for t in range(TT):
                    square_sum(norm, t)
                    if t >= 1 and norm < 4:
                        hT_parts(norm, t - 1)
                if norm < 4:
                    hT_parts(norm, TT - 1)

            square_sum(0, 0)
            split(0, 0, 0)
            square_sum(0, 1)
            hT_parts(0, 0)
            split(0, 1, 0)
            hT_parts(0, 1)
            split(0, 2, 0)
            split(0, 3, 0)
            square_sum(0, 2)
            square_sum(0, 3)
            hT_parts(0, 2)
            hT_parts(0, 3)
            act.wait_ge(wf_landed, 16)
            nc.scalar.activation(wf_split[0][:, :, :], wf[:, :, :], ACT.Copy).then_inc(wf_hi, 1)

            def exps(h, tbs):
                for tb in tbs:
                    c = ORDER.index(tb)
                    act.wait_ge(logit_ready, 4 * h + c + 1)
                    n = P * (tb + 1)
                    v = prob[:, h % 2, OFF[tb]:OFF[tb] + n]
                    pair, k = h // 2, 2 * tb + h % 2
                    nc.scalar.activation(v, v, ACT.Exp, bias=negmax[:, h % 2, c:c + 1], scale=-1.0,
                                         accum_out=den[:, pair % 2, k:k + 1]).then_inc(prob_ready, 1)

            def attention(j):
                for h, g, pair in attention_steps(j):
                    if pair is not None:
                        output_hi(pair)
                    if h is not None:
                        exps(h, (3, 2, 0))
                    if g is not None:
                        act.wait_ge(ptT_done, 3 * g + 3)
                        nc.scalar.activation(probT[:, OFF[1]:OFF[1] + 256], bank[4 + (3 * g + 2) % 2][:, 0:256],
                                             ACT.Copy).then_inc(pt_c, 1)
                    if h is not None:
                        exps(h, (1,))
                if j in TURN_AFTER_JOB:
                    output_hi(TURN_AFTER_JOB[j])

            def output_hi(pair):
                act.wait_ge(oT_done, pair + 1)
                nc.scalar.activation(oT[0][:, pair, :], bank[7][:, :], ACT.Copy).then_inc(oT_hi, 1)

            for n, (kind, i) in enumerate(E_PANELS):
                for q in range(4):
                    j = e_first_job(n) + q
                    split(n + 1, q, (n + 1) % 2, e_first_job(n) if q == 0 else None)
                    if kind == "v":
                        act.wait_ge(job_done, j + 1)
                        if i == 1:
                            act.wait_ge(pv_done, 8)
                        nc.scalar.activation(v_sb[:, q, :], bank[j % 2][:, :], ACT.Copy).then_inc(aev, 1)
                    late = kind == "qk" and i == 3 and q % 2 == 0
                    if late:
                        attention(j)
                    if kind == "qk":
                        pair, which = 2 * i + q // 2, q % 2
                        act.wait_ge(job_done, j + 1)
                        if pair >= 2:
                            act.wait_ge(score_done, 6 * (pair - 1))
                        nc.scalar.activation(qk_sb[:, pair % 2, which, :], bank[j % 2][:, :], ACT.Copy,
                                             scale=HD ** -0.5 if which == 0 else 1.0).then_inc(aev, 1)
                    if not late:
                        attention(j)
                if n == 0:
                    act.wait_ge(gate_abs, 1)
                    nc.scalar.activation(gate[:, 2, :], gate[:, 1, :], ACT.Exp, scale=-1.0).then_inc(gate_exp, 1)
                    act.wait_ge(gate_exp, 1)
                    nc.scalar.activation(gate[:, 1, :], gate[:, 2, :], ACT.Ln, bias=1.0).then_inc(gate_ln, 1)

            def mlp(c, pan, jobs, hids, last=False, first=False):
                for j in range(8):
                    parity = first_bank(jobs, j) if first else (jobs + j) % 2
                    n = 4 * c + j // 4
                    split(pan + n + 1, j % 4, (j // 4 + 1) % 2, jobs + 16 * c + j if j % 4 == 0 else None)
                    act.wait_ge(job_done, jobs + 16 * c + j + 1)
                    nc.scalar.activation(relu_sb[:, j % 2, :], bank[parity][:, :], ACT.Relu).then_inc(aev, 1)
                    act.wait_ge(sq_ready, hids + 8 * c + j + 1)
                    nc.scalar.activation(hid[0][:, j, :], sq_sb[:, j % 2, :], ACT.Copy).then_inc(hid_hi, 1)
                for q in range(8):
                    if not (last and q >= 4):
                        n = 4 * c + 2 + q // 4
                        split(pan + n + 1, q % 4, (q // 4 + 1) % 2, jobs + 16 * c + 8 + q if q % 4 == 0 else None)

            norm_tiles(1)
            mlp(0, PAN_M0, JOB_M0, 0, first=True)
            with act.Fori(1, CHUNKS) as c:
                mlp(c, PAN_M0, JOB_M0, 0)

            norm_tiles(2)

            def r_evac(h, n, s, stage, jobs):
                for q in range(4):
                    split(n + 1, q, 1 - s, jobs if q == 0 else None)
                    act.wait_ge(job_done, jobs + q + 1)
                    src = bank[first_bank(JOB_O, q) if isinstance(h, int) and stage == "qk" else (JOB_O + q) % 2][:, :]
                    if stage == "qk":
                        dst = (rq_sb if q < 2 else rk_sb)[:, q % 2, :]
                    else:
                        dst = (v_sb if stage == "v" else y_sb)[:, q, :]
                    nc.scalar.activation(dst, src, ACT.Silu if stage == "g" else ACT.Copy).then_inc(aev, 1)

            def r_scale(h):
                for t in range(4):
                    act.wait_ge(gn_r, 4 * h + t + 1)
                    act.wait_ge(y_part, 4 * h + t + 1)
                    nc.scalar.activation(y_sb[:, t, :], y_sb[:, t, :], ACT.Copy,
                                         scale=gn_rstd[:, t:t + 1]).then_inc(y_ready, 1)

            def r_turn(h):
                for k in range(4):
                    act.wait_ge(yT_done, 4 * h + k + 1)
                    nc.scalar.activation(yT[0][:, k, :], bank[2 + k % 2][:, :], ACT.Copy).then_inc(yT_hi, 1)

            def r_out_split(n, s, jobs):
                for c in range(4):
                    split(n + 1, c, 1 - s, jobs if c == 0 else None)

            r_evac(0, PAN_O, 0, "qk", JOB_O)
            r_evac(0, PAN_O + 1, 1, "v", JOB_O + 4)
            r_evac(0, PAN_O + 2, 0, "g", JOB_O + 8)
            with act.Fori(1, RH) as h:
                jb = JOB_O - 8 + 20 * h
                r_scale(h - 1)
                r_evac(h, PAN_O - 1 + 4 * h, 1, "qk", jb)
                r_turn(h - 1)
                r_out_split(PAN_O + 4 * h, 0, jb + 4)
                r_evac(h, PAN_O + 1 + 4 * h, 1, "v", jb + 12)
                r_evac(h, PAN_O + 2 + 4 * h, 0, "g", jb + 16)
            r_scale(RH - 1)
            r_turn(RH - 1)
            r_out_split(PAN_O + 15, 1, JOB_O + 72)

            norm_tiles(3)
            mlp(0, PAN_M1, JOB_M1, 32, first=True)
            with act.Fori(1, CHUNKS - 1) as c:
                mlp(c, PAN_M1, JOB_M1, 32)
            mlp(CHUNKS - 1, PAN_M1, JOB_M1, 32, last=True)
            norm_tiles(4)

        @block.vector
        def _(dve):
            def split(n, c, slot):
                dve.wait_ge(hi_split, 4 * n + c + 1)
                nc.vector.tensor_tensor(slots[slot][1][:, 2 * c:2 * c + 2, :], raw[:, c],
                                        slots[slot][0][:, 2 * c:2 * c + 2, :].bitcast(F32),
                                        ALU.subtract).then_inc(lo_split, 1)

            def variance(norm, t):
                dve.wait_ge(ss_ready, 4 * norm + t + 1)
                nc.vector.tensor_scalar(var[:, t:t + 1], ssum[:, t:t + 1], 1.0 / D, EPS, ALU.mult,
                                        ALU.add).then_inc(var_ready, 1)

            def normed(norm, t):
                if t == 0:
                    dve.wait_ge(gain_landed, 16 * (norm + 1))
                dve.wait_ge(rstd_ready, 4 * norm + t + 1)
                if norm < 4 and t >= 2:
                    dve.wait_ge(xnT_done, 8 * norm + 2 * (t - 2) + 2)
                if norm == 4 and t >= 2:
                    dve.wait_ge(out_saved[t % 2], 16)
                nc.vector.scalar_tensor_tensor(out=xn[:, t % 2, :], in0=x[:, t, :], scalar=rstd[:, t:t + 1],
                                               in1=gain[:, :], op0=ALU.mult, op1=ALU.mult).then_inc(xn_ready, 1)

            def hT_parts(norm, t):
                for b in range(2):
                    dve.wait_ge(hT_hi, 8 * norm + 2 * t + b + 1)
                    hi = hT[0][:, 4 * b:4 * b + 4, P * t:P * t + P].bitcast(F32)
                    nc.vector.tensor_tensor(hT[1][:, 4 * b:4 * b + 4, P * t:P * t + P],
                                            bank[4 + 2 * (t % 2) + b][:, :].rearrange("p (k n) -> p k n", k=4),
                                            hi, ALU.subtract).then_inc(hT_lo, 1)

            def residual(parity, f, t, jobs_done):
                dve.wait_ge(job_done, jobs_done)
                v = x[:, t, 512 * f:512 * f + 512]
                nc.vector.tensor_tensor(v, bank[parity][:, :], v, ALU.add).then_inc(dev, 1)

            def norm_tiles(norm, last_residual=None):
                for t in range(TT):
                    if last_residual is not None:
                        last_residual(t)
                    variance(norm, t)
                    normed(norm, t)
                    if t >= 1 and norm < 4:
                        hT_parts(norm, t - 1)
                if norm < 4:
                    hT_parts(norm, TT - 1)

            def norm_of(t):
                variance(0, t)
                normed(0, t)

            norm_of(0)
            split(0, 0, 0)
            norm_of(1)
            hT_parts(0, 0)
            split(0, 1, 0)
            hT_parts(0, 1)
            split(0, 2, 0)
            split(0, 3, 0)
            norm_of(2)
            norm_of(3)
            hT_parts(0, 2)
            hT_parts(0, 3)
            dve.wait_ge(ident_landed, 16)
            dve.wait_ge(const_landed, 16 * 4)
            nc.vector.tensor_copy(ident_bf[:, :], ident[:, :]).then_inc(consts_made, 1)
            nc.vector.tensor_copy(causal_bf[:, :], causal).then_inc(consts_made, 1)
            dve.wait_ge(wf_hi, 1)
            nc.vector.tensor_tensor(wf_split[1][:, :, :], wf[:, :, :], wf_split[0][:, :, :].bitcast(F32),
                                    ALU.subtract).then_inc(wf_lo, 1)

            def logits(h, u):
                if h == 0 and u == 0:
                    dve.wait_ge(negc_ready, 1)
                if u == 0:
                    if h < 8:
                        dve.wait_ge(table_ready, h + 1)
                    else:
                        dve.wait_ge(bias_landed[h % 2], 16 * ((h - 8) // 2 + 1))
                dve.wait_ge(score_done, 3 * h + u + 1)
                col = 0
                for tb in UNITS[u]:
                    n = P * (tb + 1)
                    c = ORDER.index(tb)
                    tab = table[:, h % 2, S - n:S] if h < 8 else table[:, h % 2, 0:n]
                    if h >= 2:
                        dve.wait_ge(prob_ready, 4 * (h - 2) + c + 1)
                    nc.vector.tensor_tensor_reduce(
                        out=prob[:, h % 2, OFF[tb]:OFF[tb] + n], in0=bank[2 + (3 * h + u) % 2][:, col:col + n],
                        in1=tab, scale=-1.0, scalar=BIG, op0=ALU.add, op1=ALU.min,
                        accum_out=negmax[:, h % 2, c:c + 1]).then_inc(logit_ready, 1)
                    col += n

            def copy_probT(g, u):
                dve.wait_ge(ptT_done, 3 * g + u + 1)
                o = OFF[UNITS[u][0]]
                nc.vector.tensor_copy(probT[:, o:o + 512], bank[4 + (3 * g + u) % 2][:, :]).then_inc(pt_ab, 1)

            def normalise(pair):
                dve.wait_ge(prob_ready, 8 * (pair + 1))
                if pair == 0:
                    dve.wait_ge(negc_saved, 16)
                if pair:
                    dve.wait_ge(oT_done, pair)
                    dve.wait_ge(o_norm, pair)
                nc.vector.reciprocal(rden[:, :], den[:, pair % 2, :]).then_inc(rden_ready, 1)
                dve.wait_ge(rden_ready, pair + 1)
                dve.wait_ge(pv_done, 2 * (pair + 1))
                nc.vector.tensor_tensor(o_sb.rearrange("p (k n) -> p k n", k=8),
                                        bank[6][:, :].rearrange("p (k n) -> p k n", k=8),
                                        rden[:, :].rearrange("p (k o) -> p k o", o=1).to_broadcast([P, 8, HD]),
                                        ALU.mult).then_inc(o_norm, 1)

            def output_lo(pair):
                dve.wait_ge(oT_hi, pair + 1)
                nc.vector.tensor_tensor(oT[1][:, pair, :], bank[7][:, :], oT[0][:, pair, :].bitcast(F32),
                                        ALU.subtract).then_inc(oT_lo, 1)

            def attention(j):
                for h, g, pair in attention_steps(j):
                    if pair is not None:
                        output_lo(pair)
                    for u in range(3):
                        if h is not None:
                            logits(h, u)
                        if g is not None and u < 2:
                            copy_probT(g, u)
                    if g is not None and g % 2 == 1:
                        normalise(g // 2)
                if j in TURN_AFTER_JOB:
                    output_lo(TURN_AFTER_JOB[j])

            for n, (kind, i) in enumerate(E_PANELS):
                for q in range(4):
                    j = e_first_job(n) + q
                    split(n + 1, q, (n + 1) % 2)
                    if kind == "out":
                        if i == 0:
                            residual(j % 2, 0, q, j + 1)
                    else:
                        attention(j)
                    if kind == "out" and i == 1:
                        residual(j % 2, 1, q, j + 1)
                        variance(1, q)
                        normed(1, q)
                        if q >= 1:
                            hT_parts(1, q - 1)
                if n == 0:
                    dve.wait_ge(job_done, GATE_JOB + 1)
                    nc.vector.tensor_scalar(gate[:, 0, :], bank[GATE_JOB % 2][0:NFOX, :], bias_f[:, 0:1], None,
                                            ALU.add).then_inc(dev, 1)
                    dve.wait_ge(dev, 1)
                    nc.vector.scalar_tensor_tensor(out=gate[:, 1, :], in0=gate[:, 0, :], scalar=-1.0, in1=gate[:, 0, :],
                                                   op0=ALU.mult, op1=ALU.max).then_inc(gate_abs, 1)
                    nc.vector.tensor_scalar(gate[:, 3, :], gate[:, 0, :], 0.0, None, ALU.min).then_inc(gate_min, 1)
                    dve.wait_ge(gate_min, 1)
                    dve.wait_ge(gate_ln, 1)
                    nc.vector.tensor_tensor_scan(negc, gate[:, 1, :], gate[:, 3, :], 0.0, ALU.add,
                                                 ALU.subtract).then_inc(negc_ready, 1)
            hT_parts(1, TT - 1)

            def mlp(c, pan, jobs, avs, hids, norm=None):
                for j in range(8):
                    split(pan + 4 * c + j // 4 + 1, j % 4, (j // 4 + 1) % 2)
                    dve.wait_ge(hid_lo, hids + 8 * c + j - 1) if (hids or j >= 2 or not isinstance(c, int)) else None
                    dve.wait_ge(aev, avs + 8 * c + j + 1)
                    nc.vector.tensor_tensor(sq_sb[:, j % 2, :], relu_sb[:, j % 2, :], relu_sb[:, j % 2, :],
                                            ALU.mult).then_inc(sq_ready, 1)
                    dve.wait_ge(hid_hi, hids + 8 * c + j + 1)
                    nc.vector.tensor_tensor(hid[1][:, j, :], sq_sb[:, j % 2, :], hid[0][:, j, :].bitcast(F32),
                                            ALU.subtract).then_inc(hid_lo, 1)
                for q in range(8):
                    if not (norm == 4 and q >= 4):
                        split(pan + 4 * c + 3 + q // 4, q % 4, (q // 4 + 1) % 2)
                    residual((jobs + q) % 2, q // 4, q % 4, jobs + 16 * c + 8 + q + 1)
                    if norm is not None and q >= 4:
                        t = q % 4
                        variance(norm, t)
                        normed(norm, t)
                        if t >= 1 and norm < 4:
                            hT_parts(norm, t - 1)
                if norm is not None and norm < 4:
                    hT_parts(norm, TT - 1)

            mlp(0, PAN_M0, JOB_M0, AEV_M0, 0)
            with dve.Fori(1, CHUNKS - 1) as c:
                mlp(c, PAN_M0, JOB_M0, AEV_M0, 0)
            mlp(CHUNKS - 1, PAN_M0, JOB_M0, AEV_M0, 0, norm=2)

            def r_split(n, s):
                for c in range(4):
                    split(n + 1, c, 1 - s)

            def r_decay(h, table_row):
                for s in range(4):
                    n = S - P * s
                    dve.wait_ge(rs_done, 4 * h + s + 1)
                    nc.vector.tensor_tensor(att[:, ATT_OFF[s]:ATT_OFF[s] + n], bank[2 + s % 2][:, 0:n],
                                            table_row(n), ALU.mult).then_inc(att_ready, 1)

            def r_norm(h):
                def stats(t):
                    nc.vector.bn_stats(gn_stats[:, t, :], bank[4 + t][:, :]).then_inc(gn_st, 1)

                def aggregate(t):
                    nc.vector.bn_aggr(gn_mv[:, t, :], gn_stats[:, t, :]).then_inc(gn_ag, 1)

                dve.wait_ge(ro_done, 4 * h + 1)
                stats(0)
                dve.wait_ge(ro_done, 4 * h + 2)
                dve.wait_ge(gn_st, 4 * h + 1)
                stats(1)
                aggregate(0)
                for t in range(4):
                    dve.wait_ge(gn_ag, 4 * h + t + 1)
                    if t < 2:
                        dve.wait_ge(ro_done, 4 * h + t + 3)
                        dve.wait_ge(gn_st, 4 * h + t + 2)
                        stats(t + 2)
                    if t == 2:
                        dve.wait_ge(gn_st, 4 * h + 4)
                    nc.vector.tensor_scalar(gn_var[:, t:t + 1], gn_mv[:, t, 1:2], EPS, None, ALU.add).then_inc(gn_v, 1)
                    if t < 3:
                        aggregate(t + 1)
                    dve.wait_ge(aev, AEV_O + 12 * h + 8 + t + 1)
                    nc.vector.scalar_tensor_tensor(out=y_sb[:, t, :], in0=bank[4 + t][:, :], scalar=gn_mv[:, t, 0:1],
                                                   in1=y_sb[:, t, :], op0=ALU.subtract,
                                                   op1=ALU.mult).then_inc(y_part, 1)

            def r_turn(h):
                for k in range(4):
                    dve.wait_ge(yT_hi, 4 * h + k + 1)
                    nc.vector.tensor_tensor(yT[1][:, k, :], bank[2 + k % 2][:, :], yT[0][:, k, :].bitcast(F32),
                                            ALU.subtract).then_inc(yT_lo, 1)

            def r_out(n, s, jobs, norm=None):
                for q in range(8):
                    if q % 2 == 0:
                        split(n + 1, q // 2, 1 - s)
                    residual((JOB_O + q) % 2, q // 4, q % 4, jobs + q + 1)
                    if norm is not None and q >= 4:
                        t = q % 4
                        variance(norm, t)
                        normed(norm, t)
                        if t >= 1:
                            hT_parts(norm, t - 1)
                if norm is not None:
                    hT_parts(norm, TT - 1)

            dve.wait_ge(decay_landed, 16)
            r_split(PAN_O, 0)
            r_split(PAN_O + 1, 1)
            r_decay(0, lambda n: decay[:, 0, 0:n])
            r_split(PAN_O + 2, 0)
            r_norm(0)
            with dve.Fori(1, RH) as h:
                jb = JOB_O - 8 + 20 * h
                r_split(PAN_O - 1 + 4 * h, 1)
                r_turn(h - 1)
                r_out(PAN_O + 4 * h, 0, jb + 4)
                r_split(PAN_O + 1 + 4 * h, 1)
                r_decay(h, lambda n: decay[:, bass.ds(h, 1), 0:n].rearrange("p a n -> p (a n)"))
                r_split(PAN_O + 2 + 4 * h, 0)
                r_norm(h)
            r_turn(RH - 1)
            r_out(PAN_O + 15, 1, JOB_O + 72, norm=3)

            with dve.Fori(0, CHUNKS - 1) as c:
                mlp(c, PAN_M1, JOB_M1, AEV_M1, 32)
            mlp(CHUNKS - 1, PAN_M1, JOB_M1, AEV_M1, 32, norm=4)

        @block.gpsimd
        def _(pool):
            nc.gpsimd.memset(half_neg[:, :], -0.5).then_inc(half_made, 1)

            def load_gain(norm):
                if norm:
                    pool.wait_ge(xn_ready, 4 * norm)
                pool.dma_start(gain[:, :], gains[norm].to_broadcast([P, D])).then_inc(gain_landed, 16)

            def inv_std(norm):
                for t in range(TT):
                    pool.wait_ge(var_ready, 4 * norm + t + 1)
                    nc.gpsimd.tensor_tensor(rstd[:, t:t + 1], var[:, t:t + 1], half_neg[:, :],
                                            ALU.pow).then_inc(rstd_ready, 1)

            load_gain(0)
            pool.wait_ge(half_made, 1)
            inv_std(0)
            load_gain(1)

            for h in range(8):
                if h == 0:
                    pool.wait_ge(consts_made, 2)
                if h >= 2:
                    pool.wait_ge(logit_ready, 4 * (h - 1))
                nc.gpsimd.tensor_scalar(table[:, h % 2, :], delta, -(2.0 ** -(h + 1)), None,
                                        ALU.mult).then_inc(table_tmp, 1)
                pool.wait_ge(table_tmp, h + 1)
                nc.gpsimd.tensor_tensor(table[:, h % 2, :], table[:, h % 2, :], lncount, ALU.add).then_inc(table_ready, 1)
                if h == 1:
                    pool.wait_ge(negc_ready, 1)
                    pool.dma_start(negc_dram, negc).then_inc(negc_saved, 16)
            pool.wait_ge(negc_saved, 16)
            for h in range(8, 16):
                pool.wait_ge(logit_ready, 4 * (h - 1))
                pool.dma_start(table[:, h % 2, :], negc_dram[h - 8:h - 7, :].to_broadcast([P, S])
                               ).then_inc(bias_landed[h % 2], 16)
            inv_std(1)
            load_gain(2)
            pool.dma_start(decay, c_decay).then_inc(decay_landed, 16)
            inv_std(2)
            load_gain(3)

            def gn_inv_std(h):
                for t in range(4):
                    pool.wait_ge(gn_v, 4 * h + t + 1)
                    nc.gpsimd.tensor_tensor(gn_rstd[:, t:t + 1], gn_var[:, t:t + 1], half_neg[:, :],
                                            ALU.pow).then_inc(gn_r, 1)

            with pool.Fori(0, RH) as h:
                gn_inv_std(h)
            inv_std(3)
            load_gain(4)
            inv_std(4)


_INS = ["x", "norm_mix_g", "norm_ffn_g", "even_w_in", "even_b_f", "even_w_out", "odd_w_in", "odd_w_out",
        "ffn_w_in", "ffn_w_out", "final_g"]


def constants():
    p = np.arange(P)[:, None]
    j = np.arange(S)[None, :]
    eye = np.eye(P, dtype=np.float32)
    causal = np.where(np.arange(P)[None, :] > p, NEG, 0.0).astype(np.float32)
    dist = p + (S - P) - j
    count = (dist >= 0) * ((dist <= 128) * 1 + (dist % 4 == 0) + (dist % 16 == 0))
    lncount = np.where(count > 0, np.log(np.maximum(count, 1)), NEG).astype(np.float32)
    gamma = 1.0 - 2.0 ** (-5.0 - np.arange(RH, dtype=np.float32))
    log_g = np.log(gamma.astype(np.float32)).astype(np.float64)
    rel = j - p
    decay = np.where(rel[:, None, :] >= 0, np.exp(log_g[None, :, None] * np.maximum(rel, 0)[:, None, :]), 0.0) / 16.0
    return {"c_ident": eye, "c_causal": causal, "c_delta": np.maximum(dist, 0).astype(np.float32),
            "c_lncount": lncount, "c_decay": decay.astype(np.float32)}


def kernel(**inputs):
    import concourse.bacc as _bacc
    from concourse.bass_utils import run_bass_kernel_spmd as _run

    nc = _bacc.Bacc("TRN2", target_bir_lowering=False, num_devices=1)
    arrays, args = {}, []
    for name, a in [(n, inputs[n]) for n in _INS] + list(constants().items()):
        a = np.ascontiguousarray(a)
        arrays[f"in_{name}"] = a
        args.append(nc.dram_tensor(f"in_{name}", a.shape, mybir.dt.from_np(a.dtype), kind="ExternalInput").ap())
    args.append(nc.dram_tensor("out_0", (1, S, D), F32, kind="ExternalOutput").ap())
    negc_dram = nc.dram_tensor("negc_dram", (NFOX, S), F32, kind="Internal").ap()
    trunk(nc, *args, negc_dram)
    r = _run(nc, [arrays], core_ids=[0])
    return r.results[0]["out_0"]
```

```python
from contextlib import ExitStack

import numpy as np

import concourse.bass as bass
from concourse import mybir

F32 = mybir.dt.float32
F32R = mybir.dt.float32r
BF16 = mybir.dt.bfloat16
ALU = mybir.AluOpType
ACT = mybir.ActivationFunctionType

P = 128
S = 512
D = 1024
TT = S // P
KT = D // P
HD = 64
WA = 512
NPAIR = 8
NHEAD = 16
NFOX = 8
RH = 4
RV = 512
HID = 4096
CHUNKS = HID // D
EPS = 1e-6
PASSES = ((0, 0), (0, 1), (1, 0))
NEG = -1e30
BIG = 3.0e38

PAN_E, PAN_M0, PAN_O, PAN_M1, PANELS = 0, 8, 24, 40, 56
JOB_E, JOB_M0, JOB_O, JOB_M1 = 0, 33, 97, 177
AEV_M0, AEV_O, AEV_M1 = 24, 56, 104
LEV_O = 16
DEV_M0, DEV_O, DEV_M1 = 9, 41, 73
DEV_END = 105

E_PANELS = [("v", 0), ("qk", 0), ("qk", 1), ("qk", 2), ("v", 1), ("qk", 3), ("out", 0), ("out", 1)]
GATE_JOB = 4


def first_bank(jobs, q):
    return 2 + q if q < 2 else (jobs + q) % 2


def e_first_job(n):
    return 4 * n + (1 if n >= 1 else 0)


def e_job_of(pair, which):
    panel = {0: 1, 1: 2, 2: 3, 3: 5}[pair // 2]
    return e_first_job(panel) + 2 * (pair % 2) + which


def e_lev(job):
    return e_aev(job) - (4 if job < e_first_job(4) else 8)


def e_aev(job):
    return job + 1 if job < GATE_JOB else job


STEPS = {7: [(0, None, None, None)],
         8: [(1, 0, None, None)],
         9: [(2, 1, 0, None)],
         10: [(3, 2, 1, None)],
         11: [(4, 3, 2, 0)],
         12: [(5, 4, 3, None)],
         13: [(6, 5, 4, 1)],
         14: [(7, 6, 5, None)],
         15: [(None, 7, 6, 2)],
         16: [(None, None, 7, None)],
         17: [(None, None, None, 3)],
         18: [(8, None, None, None)],
         19: [(9, 8, None, None)],
         21: [(10, 9, 8, None)],
         22: [(11, 10, 9, None)],
         23: [(12, 11, 10, 4)],
         24: [(13, 12, 11, None), (14, 13, 12, 5), (15, 14, 13, None)]}
TAIL = [(None, 15, 14, 6), (None, None, 15, None), (None, None, None, 7)]
EARLY_KT = 6
PT_BY_SCALAR = (False, False, True)
UNITS = ((3,), (2, 0), (1,))
ORDER = (3, 2, 0, 1)
OFF = {3: 0, 2: 512, 0: 896, 1: 1024}


def pt_count(h, u):
    mine = [v for v in range(3) if PT_BY_SCALAR[v] == PT_BY_SCALAR[u]]
    return PT_BY_SCALAR[u], len(mine) * h + mine.index(u) + 1


def out_bank(j):
    return {27: 2, 28: 3}.get(j, j % 2)


def trunk(nc, x_in, norm_mix_g, norm_ffn_g, even_w_in, even_b_f, even_w_out, odd_w_in, odd_w_out,
          ffn_w_in, ffn_w_out, final_g, c_ident, c_causal, c_delta, c_lncount, c_decay, out, negc_dram):
    gains = [norm_mix_g[0:1, :], norm_ffn_g[0:1, :], norm_mix_g[1:2, :], norm_ffn_g[1:2, :],
             final_g.rearrange("(a d) -> a d", a=1)]
    x_tiles = x_in.rearrange("b (t p) d -> (b t) p d", p=P)
    out_tiles = out.rearrange("b (t p) d -> (b t) p d", p=P)
    w_even = even_w_in[0]
    w_eout = even_w_out[0]
    w_odd = odd_w_in[0]
    w_oout = odd_w_out[0]

    with ExitStack() as ctx:
        def sb(name, shape, dt=F32):
            return ctx.enter_context(nc.sbuf_tensor(name, shape, dt))

        def sem(name):
            return ctx.enter_context(nc.semaphore(name))

        slots = [[sb(f"w_{part}{s}", [P, 8, 512], F32R) for part in ("hi", "lo")] for s in range(2)]
        raw = sb("raw", [P, 4, 2, 512])
        x = sb("x", [P, TT, D])
        hT = [sb(f"hT_{part}", [P, KT, S], F32R) for part in ("hi", "lo")]
        gain = sb("gain", [P, D])
        arena_at = nc.sbuf_base
        arena = sb("arena", [P, 10752])
        arena_r_at = nc.sbuf_base
        arena_r = sb("arena_r", [P, 16, S], F32R)
        arena_q = nc.alloc_sbuf_tensor_at("arena_q", [P, 10752], F32R, offset=arena_at)
        arena_f = nc.alloc_sbuf_tensor_at("arena_f", [P, 1024], F32, offset=arena_r_at)
        ident = sb("ident", [P, P])
        ident_bf = sb("ident_bf", [P, P], BF16)
        causal_bf = sb("causal_bf", [P, P], BF16)
        bias_f = sb("bias_f", [NFOX, 1])
        negmax = sb("negmax", [P, 2, 4])
        den = sb("den", [P, 2, 8])
        rden = sb("rden", [P, 8])
        ssum = sb("ssum", [P, 4])
        var = sb("var", [P, 4])
        rstd = sb("rstd", [P, 4])
        half_neg = sb("half_neg", [P, 1])
        gn_stats = sb("gn_stats", [P, 4, 6])
        gn_mv = sb("gn_mv", [P, 4, 2])
        gn_var = sb("gn_var", [P, 4])
        gn_rstd = sb("gn_rstd", [P, 4])

        wf = arena_f[:, 0:KT * NFOX].rearrange("p (k n) -> p k n", k=KT)
        wf_split = [arena_q[:, 4096 - 128 * (2 - a) // 2:4096 - 128 * (1 - a) // 2].rearrange("p (k n) -> p k n", k=KT)
                    for a in range(2)]
        v_sb = x[:, 0:2, :].rearrange("p a (b n) -> p (a b) n", b=2)
        qk_parts = arena_q[:, 0:4096].rearrange("p (a s w n) -> p a s w n", a=2, s=2, w=2)
        prob = arena[:, 4096:6656].rearrange("p (s n) -> p s n", s=2)
        probT = arena[:, 6656:7936]
        table = arena[:, 7936:8960].rearrange("p (s n) -> p s n", s=2)
        delta = arena[:, 8960:9472]
        lncount = arena[:, 9472:9984]
        o_sb = arena[:, 9984:10496]
        gate = arena[0:NFOX, 4096:6144].rearrange("p (s n) -> p s n", s=4)
        negc = o_sb[0:NFOX, :]
        causal = table[:, 0, 0:P]
        xn = arena[:, 4096:6144].rearrange("p (s n) -> p s n", s=2)
        junk = arena[:, 6656:7680]
        relu_sb = arena[:, 0:1024].rearrange("p (s n) -> p s n", s=2)
        sq_sb = arena[:, 1024:2048].rearrange("p (s n) -> p s n", s=2)
        rq_parts = arena_q[:, 0:4096].rearrange("p (a w k n) -> p a w k n", a=2, w=2, k=2)
        att_parts = arena_q[:, 4096:6656].rearrange("p (a n) -> p a n", a=2)
        att_tmp = arena_f[:, :].rearrange("p (s n) -> p s n", s=2)
        y_sb = arena[:, 6656:8704].rearrange("p (t n) -> p t n", t=TT)
        decay = arena[:, 8704:10752].rearrange("p (h n) -> p h n", h=RH)
        rv_parts = [arena_r[:, 8:12, :], arena_r[:, 12:16, :]]
        ATT_OFF = (0, 512, 896, 1152)
        oT = [arena_r[:, 0:8, :], arena_r[:, 8:16, :]]
        hid = oT
        yT = [arena_r[:, 0:4, :], arena_r[:, 4:8, :]]

        bank = [ctx.enter_context(nc.psum_tensor(f"bank{i}", [P, 512], F32)) for i in range(8)]

        raw_landed = [sem(f"raw_landed{c}") for c in range(4)]
        hi_split = sem("hi_split")
        lo_split = sem("lo_split")
        job_done = sem("job_done")
        aev = sem("aev")
        lev = sem("lev")
        dev = sem("dev")
        x_landed = [sem(f"x_landed{t}") for t in range(TT)]
        ident_landed = sem("ident_landed")
        const_landed = sem("const_landed")
        wf_landed = sem("wf_landed")
        gain_landed = sem("gain_landed")
        decay_landed = sem("decay_landed")
        consts_made = sem("consts_made")
        half_made = sem("half_made")
        wf_hi = sem("wf_hi")
        wf_lo = sem("wf_lo")
        ss_ready = sem("ss_ready")
        var_ready = sem("var_ready")
        rstd_ready = sem("rstd_ready")
        xn_ready = sem("xn_ready")
        xnT_done = sem("xnT_done")
        hT_hi = sem("hT_hi")
        hT_lo = sem("hT_lo")
        gate_z = sem("gate_z")
        gate_abs = sem("gate_abs")
        gate_min = sem("gate_min")
        gate_exp = sem("gate_exp")
        gate_ln = sem("gate_ln")
        negc_ready = sem("negc_ready")
        negc_saved = sem("negc_saved")
        table_tmp = sem("table_tmp")
        table_ready = sem("table_ready")
        bias_landed = [sem(f"bias_landed{i}") for i in range(2)]
        score_done = sem("score_done")
        logit_ready = sem("logit_ready")
        prob_ready = sem("prob_ready")
        ptT_done = sem("ptT_done")
        pt_v = sem("pt_v")
        pt_s = sem("pt_s")
        pv_done = sem("pv_done")
        rden_ready = sem("rden_ready")
        o_norm = sem("o_norm")
        oT_done = sem("oT_done")
        oT_hi = sem("oT_hi")
        oT_lo = sem("oT_lo")
        sq_ready = sem("sq_ready")
        hid_hi = sem("hid_hi")
        hid_lo = sem("hid_lo")
        rs_done = sem("rs_done")
        att_prod = sem("att_prod")
        att_hi = sem("att_hi")
        att_ready = sem("att_ready")
        ro_done = sem("ro_done")
        gn_st = sem("gn_st")
        gn_ag = sem("gn_ag")
        gn_v = sem("gn_v")
        gn_r = sem("gn_r")
        y_part = sem("y_part")
        y_ready = sem("y_ready")
        yT_done = sem("yT_done")
        yT_hi = sem("yT_hi")
        yT_lo = sem("yT_lo")
        out_saved = [sem(f"out_saved{i}") for i in range(2)]

        block = ctx.enter_context(nc.Block())

        @block.sync
        def _(sp):
            def load_x(t):
                sp.dma_start(x[:, t, :], x_tiles[t]).then_inc(x_landed[t], 16)

            def quarter(n, c, srcs):
                if not (isinstance(n, int) and n == 0):
                    sp.wait_ge(lo_split, 4 * n + c - 3)
                for e, src in enumerate(srcs):
                    dst = raw[:, c, e, :]
                    if len(src.shape) == 3:
                        dst = dst.rearrange("p (w n) -> p w n", w=2)
                    sp.dma_start(dst, src).then_inc(raw_landed[c], 16)

            def plain(w, r0, c0):
                return [w[bass.ds(r0 + P * k, P), bass.ds(c0, 512)] for k in range(KT)]

            def query_key(w, c0, width):
                return [w[P * k:P * k + P, bass.ds(c0, 2 * width)].rearrange("p (w n) -> p w n", w=2)[:, :, 0:256]
                        for k in range(KT)]

            def panel(n, srcs):
                for c in range(4):
                    quarter(n, c, srcs[2 * c:2 * c + 2])

            def e_panel(n):
                kind, i = E_PANELS[n]
                if kind == "v":
                    return plain(w_even, 0, 3 * WA * i + 2 * WA)
                if kind == "qk":
                    return query_key(w_even, 3 * WA * (i // 2) + 256 * (i % 2), WA)
                return plain(w_eout, 0, 512 * i)

            load_x(0)
            sp.dma_start(ident[:, :], c_ident).then_inc(ident_landed, 16)
            first = e_panel(0)
            quarter(0, 0, first[0:2])
            load_x(1)
            for c in range(1, 4):
                quarter(0, c, first[2 * c:2 * c + 2])
            load_x(2)
            load_x(3)
            with nc.allow_non_contiguous_dma(reason="eight biases, one a partition"):
                for dst, src in ((causal, c_causal), (delta, c_delta), (lncount, c_lncount),
                                 (bias_f[:, :], even_b_f.rearrange("a f -> f a"))):
                    sp.dma_start(dst, src).then_inc(const_landed, 16)
            sp.dma_start(wf[:, :, :], w_even[:, 6 * WA:6 * WA + NFOX].rearrange("(k p) n -> p k n", p=P)
                         ).then_inc(wf_landed, 16)
            for n in range(1, PAN_M0):
                panel(n, e_panel(n))
            sp.wait_ge(pv_done, NHEAD)
            for t in range(2):
                load_x(t)

            def mlp(layer, base, c):
                w1, w2 = ffn_w_in[layer], ffn_w_out[layer]
                for e in range(2):
                    panel(base + 4 * c + e, plain(w1, 0, 1024 * c + 512 * e))
                for e in range(2):
                    panel(base + 4 * c + 2 + e, plain(w2, 1024 * c, 512 * e))

            with sp.Fori(0, CHUNKS) as c:
                mlp(0, PAN_M0, c)

            def head_qk(h):
                v = w_odd[:, 0:2 * D].rearrange("r (w n) -> r w n", w=2)
                return [v[P * k:P * k + P, :, bass.ds(256 * h, 256)] for k in range(KT)]

            def head_out(h):
                return [w_oout[bass.ds(512 * h + P * c, P), 512 * f:512 * f + 512] for c in range(4) for f in range(2)]

            panel(PAN_O, head_qk(0))
            panel(PAN_O + 1, plain(w_odd, 0, 2 * D))
            panel(PAN_O + 2, plain(w_odd, 0, 4 * D))
            with sp.Fori(1, RH) as h:
                panel(PAN_O - 1 + 4 * h, head_qk(h))
                panel(PAN_O + 4 * h, head_out(h - 1))
                panel(PAN_O + 1 + 4 * h, plain(w_odd, 0, 2 * D + 512 * h))
                panel(PAN_O + 2 + 4 * h, plain(w_odd, 0, 4 * D + 512 * h))
            panel(PAN_O + 15, head_out(RH - 1))
            with sp.Fori(0, CHUNKS) as c:
                mlp(1, PAN_M1, c)
            for t in range(TT):
                sp.wait_ge(xn_ready, 16 + t + 1)
                sp.dma_start(out_tiles[t], xn[:, t % 2, :]).then_inc(out_saved[t % 2], 16)
            for i in range(2):
                sp.wait_ge(out_saved[i], 16 * TT // 2)

        @block.tensor
        def _(pe):
            def job(parity, stat, mov, slot_waits, kts=KT, first=None):
                for k in range(kts):
                    slot_waits(k)
                    for n, (a, b) in enumerate(PASSES):
                        mm = pe.matmul(bank[parity][:, :] if first is None else bank[parity][0:first, :],
                                       stat(k, a), mov(k, b),
                                       start=(k == 0 and n == 0), stop=(k == kts - 1 and n == 2))
                mm.then_inc(job_done, 1)

            def nowait(k):
                pass

            def quarter_wait(n):
                def w(k):
                    if k % 2 == 0:
                        pe.wait_ge(lo_split, 4 * n + k // 2 + 1)
                return w

            def turn_xn(norm, t):
                pe.wait_ge(xn_ready, 4 * norm + t + 1)
                for b in range(2):
                    if t >= 2:
                        pe.wait_ge(hT_lo, 8 * norm + 2 * (t - 2) + b + 1)
                    dst = bank[4 + 2 * (t % 2) + b]
                    for k in range(4):
                        mm = pe.transpose(dst[:, P * k:P * k + P],
                                          xn[:, t % 2, P * (4 * b + k):P * (4 * b + k) + P], ident[:, :])
                    mm.then_inc(xnT_done, 1)

            def first_panel(norm, n, slot):
                w = slots[slot]
                jobs, devs = {1: (JOB_M0, DEV_M0), 2: (JOB_O, DEV_O), 3: (JOB_M1, DEV_M1)}[norm]
                turn_xn(norm, 2)
                for half in range(2):
                    pe.wait_ge(hT_lo, 8 * norm + 4 * half + 4)
                    for q in range(4):
                        if half == 0 and q == 2:
                            turn_xn(norm, 3)
                            pe.wait_ge(dev, devs)
                        dst = bank[first_bank(jobs, q)]
                        c = 256 * half
                        for k in range(KT):
                            if half == 0 and q == 0 and k % 2 == 0:
                                pe.wait_ge(lo_split, 4 * n + k // 2 + 1)
                            for i, (a, b) in enumerate(PASSES):
                                mm = pe.matmul(dst[:, c:c + 256], w[a][:, k, P * q:P * q + P],
                                               hT[b][:, k, c:c + 256],
                                               start=(k == 0 and i == 0), stop=(k == KT - 1 and i == 2))
                        if half == 1:
                            mm.then_inc(job_done, 1)

            pe.wait_ge(ident_landed, 16)

            def scores_unit(h, u):
                q = 3 * h + u
                ready = ((4 * h - 1), 4 * h, 4 * h + 1)[u]
                if ready > 0:
                    pe.wait_ge(logit_ready, ready)
                if u == 0:
                    pe.wait_ge(lev, e_lev(e_job_of(h // 2, 1)))
                dst = bank[2 + q % 2]
                col = 0
                rows = slice(HD * (h % 2), HD * (h % 2) + HD)
                st = (h // 2) % 2
                fox = h >= 8
                if h == 8 and u == 0:
                    pe.wait_ge(consts_made, 2)
                for tb in UNITS[u]:
                    n = P * (tb + 1)
                    for i, (a, b) in enumerate(PASSES):
                        mm = pe.matmul(dst[:, col:col + n], qk_parts[rows, a, st, 0, P * tb:P * tb + P],
                                       qk_parts[rows, b, st, 1, 0:n], start=(i == 0), stop=(i == 2 and not fox))
                    if fox:
                        mm = pe.matmul(dst[:, col + n - P:col + n], ident_bf[:, :], causal_bf[:, :],
                                       start=False, stop=True)
                    col += n
                mm.then_inc(score_done, 1)

            def pt_wait(h, u):
                by_scalar, count = pt_count(h, u)
                pe.wait_ge(pt_s if by_scalar else pt_v, count)

            def turn_prob(h, u):
                q = 3 * h + u
                pe.wait_ge(prob_ready, 4 * h + (1, 3, 4)[u])
                if q >= 2:
                    pt_wait((q - 2) // 3, (q - 2) % 3)
                dst = bank[4 + q % 2]
                col = 0
                for tb in UNITS[u]:
                    for s in range(tb + 1):
                        mm = pe.transpose(dst[:, col:col + P], prob[:, h % 2, OFF[tb] + P * s:OFF[tb] + P * s + P],
                                          ident[:, :])
                        col += P
                mm.then_inc(ptT_done, 1)

            def gather_values(h):
                if h % 2 == 0 and h >= 2:
                    pe.wait_ge(o_norm, h // 2)
                pe.wait_ge(aev, e_aev(e_first_job(0 if h < 8 else 4) + 3))
                for u in range(3):
                    pt_wait(h, u)
                    for tb in UNITS[u]:
                        for s in range(tb + 1):
                            c = P * tb + HD * (h % 2)
                            o = OFF[tb] + P * s
                            mm = pe.matmul(bank[6][:, c:c + HD], probT[:, o:o + P],
                                           v_sb[:, s, HD * (h % 8):HD * (h % 8) + HD],
                                           start=(s == 0), stop=(s == tb))
                mm.then_inc(pv_done, 1)

            def turn_output(pair):
                pe.wait_ge(o_norm, pair + 1)
                if pair:
                    pe.wait_ge(oT_lo, pair)
                for t in range(TT):
                    mm = pe.transpose(bank[7][:, P * t:P * t + P], o_sb[:, P * t:P * t + P], ident[:, :])
                mm.then_inc(oT_done, 1)

            def step(h, g, v, pair):
                for u in range(3):
                    if h is not None:
                        scores_unit(h, u)
                    if u == 0 and v is not None:
                        gather_values(v)
                    if g is not None:
                        turn_prob(g, u)
                if pair is not None:
                    turn_output(pair)

            def out_part(j, ks):
                n = 6 + (j - e_first_job(6)) // 4
                w, t = slots[n % 2], (j - e_first_job(6)) % 4
                for k in ks:
                    if t == 0 and k % 2 == 0:
                        pe.wait_ge(lo_split, 4 * n + k // 2 + 1)
                    if j == e_first_job(6):
                        pe.wait_ge(oT_lo, k + 1)
                    for i, (a, b) in enumerate(PASSES):
                        mm = pe.matmul(bank[out_bank(j)][:, :], oT[a][:, k, P * t:P * t + P], w[b][:, k, :],
                                       start=(k == 0 and i == 0), stop=(k == KT - 1 and i == 2))
                if ks[-1] == KT - 1:
                    mm.then_inc(job_done, 1)

            def e_job_free(j):
                if j < 2:
                    return
                p = j - 2
                if p == GATE_JOB:
                    pe.wait_ge(dev, 1)
                elif p < 4 or 17 <= p < 21:
                    pe.wait_ge(aev, e_aev(p))
                elif p < 25:
                    pe.wait_ge(lev, e_lev(p))
                else:
                    pe.wait_ge(dev, 1 + p - 24)

            for n, (kind, i) in enumerate(E_PANELS[:6]):
                w = slots[n % 2]
                for q in range(4):
                    j = e_first_job(n) + q
                    if n == 0:
                        for t in ((0, 1), (2,), (3,), ())[q]:
                            turn_xn(0, t)
                        pe.wait_ge(hT_lo, 2 * (q + 1))
                    e_job_free(j)
                    waits = quarter_wait(n) if q == 0 else nowait
                    if kind == "v":
                        job(j % 2, lambda k, a: hT[a][:, k, P * q:P * q + P], lambda k, b: w[b][:, k, :], waits)
                    else:
                        c = 256 * (q % 2) + P * (q // 2)
                        job(j % 2, lambda k, a: w[a][:, k, c:c + P], lambda k, b: hT[b][:, k, :], waits)
                    for st in STEPS.get(j, []):
                        step(*st)
                if n == 0:
                    e_job_free(GATE_JOB)
                    pe.wait_ge(wf_lo, 1)
                    job(GATE_JOB % 2, lambda k, a: wf_split[a][:, k, :], lambda k, b: hT[b][:, k, :], nowait,
                        first=NFOX)
            e_job_free(25)
            out_part(25, range(EARLY_KT))
            step(*TAIL[0])
            e_job_free(26)
            out_part(26, range(EARLY_KT))
            step(*TAIL[1])
            pe.wait_ge(logit_ready, 4 * NHEAD)
            out_part(27, range(EARLY_KT))
            step(*TAIL[2])
            out_part(28, range(EARLY_KT))
            for j in range(25, 29):
                out_part(j, range(EARLY_KT, KT))
            for j in range(29, 33):
                e_job_free(j)
                out_part(j, range(KT))
                if j in (30, 31):
                    turn_xn(1, j - 30)

            def mlp(c, pan, jobs, avs, dvs, first=None, last=None):
                if first is not None:
                    first_panel(first, pan, 0)
                for j in range(0 if first is None else 4, 8):
                    w = slots[j // 4]
                    if j < 2:
                        pe.wait_ge(dev, dvs + 8 * c - 1 + j)
                    else:
                        pe.wait_ge(aev, avs + 8 * c + j - 1)
                    waits = quarter_wait(pan + 4 * c + j // 4) if j % 4 == 0 else nowait
                    col = P * (j % 4)
                    job((jobs + j) % 2, lambda k, a: w[a][:, k, col:col + P], lambda k, b: hT[b][:, k, :], waits)
                for q in range(8):
                    w = slots[q // 4]
                    if q < 2:
                        pe.wait_ge(aev, avs + 8 * c + 7 + q)
                    else:
                        pe.wait_ge(dev, dvs + 8 * c + q - 1)
                    waits = quarter_wait(pan + 4 * c + 2 + q // 4) if q % 4 == 0 else nowait

                    def both(k, waits=waits, q=q):
                        waits(k)
                        if q == 0:
                            pe.wait_ge(hid_lo, (avs_hid[jobs]) + 8 * c + k + 1)
                    t = q % 4
                    job((jobs + q) % 2, lambda k, a: hid[a][:, k, P * t:P * t + P], lambda k, b: w[b][:, k, :], both)
                    if last is not None and q in (5, 6):
                        turn_xn(last, q - 5)

            avs_hid = {JOB_M0: 0, JOB_M1: 32}
            mlp(0, PAN_M0, JOB_M0, AEV_M0, DEV_M0, first=1)
            with pe.Fori(1, CHUNKS - 1) as c:
                mlp(c, PAN_M0, JOB_M0, AEV_M0, DEV_M0)
            mlp(CHUNKS - 1, PAN_M0, JOB_M0, AEV_M0, DEV_M0, last=2)


            def r_free(h, stage, q):
                first = isinstance(h, int) and h == 0
                last = isinstance(h, int) and h == RH
                if stage == "qk":
                    if q < 2:
                        pe.wait_ge(aev, AEV_O + 12 * h - 1 + q)
                    else:
                        pe.wait_ge(lev, LEV_O + 8 * h + q - 1)
                elif stage == "out":
                    if q >= 2:
                        pe.wait_ge(dev, DEV_O + 8 * (h - 1) + q - 1)
                    elif last:
                        pe.wait_ge(aev, AEV_O + 12 * h + q - 1)
                    else:
                        pe.wait_ge(lev, LEV_O + 8 * h + 3 + q)
                elif stage == "v":
                    if q < 2 and not first:
                        pe.wait_ge(dev, DEV_O + 8 * (h - 1) + 7 + q)
                    else:
                        pe.wait_ge(lev, LEV_O + 8 * h + 3 + q)
                else:
                    if q < 2:
                        pe.wait_ge(lev, LEV_O + 8 * h + 7 + q)
                    else:
                        pe.wait_ge(aev, AEV_O + 12 * h + 7 + q)

            def r_qk(h, n, s):
                w = slots[s]
                for q in range(4):
                    r_free(h, "qk", q)
                    job((JOB_O + q) % 2, lambda k, a: w[a][:, k, P * q:P * q + P], lambda k, b: hT[b][:, k, :],
                        quarter_wait(n) if q == 0 else nowait)

            def r_vg(h, n, s, stage):
                w = slots[s]
                for q in range(4):
                    r_free(h, stage, q)
                    job((JOB_O + q) % 2, lambda k, a: hT[a][:, k, P * q:P * q + P], lambda k, b: w[b][:, k, :],
                        quarter_wait(n) if q == 0 else nowait)

            def r_scores(h):
                for s in range(4):
                    if s == 0:
                        pe.wait_ge(lev, LEV_O + 8 * h + 4)
                    if s >= 2:
                        pe.wait_ge(att_prod, 4 * h + s - 1)
                    n = S - P * s
                    for k in range(2):
                        for i, (a, b) in enumerate(PASSES):
                            mm = pe.matmul(bank[2 + s % 2][:, 0:n], rq_parts[:, a, 1, k, P * s:P * s + P],
                                           rq_parts[:, b, 0, k, P * s:S],
                                           start=(k == 0 and i == 0), stop=(k == 1 and i == 2))
                    mm.then_inc(rs_done, 1)

            def r_values(h):
                pe.wait_ge(lev, LEV_O + 8 * h + 8)
                for t in range(4):
                    pe.wait_ge(att_ready, 4 * h + t + 1)
                    for s in range(t + 1):
                        o = ATT_OFF[s] + P * (t - s)
                        for i, (a, b) in enumerate(PASSES):
                            mm = pe.matmul(bank[4 + t][:, :], att_parts[:, a, o:o + P], rv_parts[b][:, s, :],
                                           start=(s == 0 and i == 0), stop=(s == t and i == 2))
                    mm.then_inc(ro_done, 1)

            def r_turn(h):
                for k in range(4):
                    if k >= 2:
                        pe.wait_ge(yT_lo, 4 * h + k - 1)
                    for t in range(4):
                        if k == 0:
                            pe.wait_ge(y_ready, 4 * h + t + 1)
                        mm = pe.transpose(bank[2 + k % 2][:, P * t:P * t + P], y_sb[:, t, P * k:P * k + P], ident[:, :])
                    mm.then_inc(yT_done, 1)

            def r_out(h, n, s, at):
                w = [slots[s][b][:, :, :].rearrange("p (k f) n -> p k (f n)", f=2) for b in range(2)]
                for q in range(8):
                    r_free(at, "out", q)
                    f, t = q // 4, q % 4

                    def waits(k, q=q):
                        if q == 0:
                            pe.wait_ge(lo_split, 4 * n + k + 1)
                            pe.wait_ge(yT_lo, 4 * h + k + 1)
                    job((JOB_O + q) % 2, lambda k, a: yT[a][:, k, P * t:P * t + P],
                        lambda k, b: w[b][:, k, 512 * f:512 * f + 512], waits, kts=4)
                    if isinstance(at, int) and q in (6, 7):
                        turn_xn(3, q - 6)

            first_panel(2, PAN_O, 0)
            r_vg(0, PAN_O + 1, 1, "v")
            r_scores(0)
            r_vg(0, PAN_O + 2, 0, "g")
            r_values(0)
            with pe.Fori(1, RH) as h:
                r_qk(h, PAN_O - 1 + 4 * h, 1)
                r_turn(h - 1)
                r_out(h - 1, PAN_O + 4 * h, 0, h)
                r_vg(h, PAN_O + 1 + 4 * h, 1, "v")
                r_scores(h)
                r_vg(h, PAN_O + 2 + 4 * h, 0, "g")
                r_values(h)
            r_turn(RH - 1)
            r_out(RH - 1, PAN_O + 15, 1, RH)

            mlp(0, PAN_M1, JOB_M1, AEV_M1, DEV_M1, first=3)
            with pe.Fori(1, CHUNKS) as c:
                mlp(c, PAN_M1, JOB_M1, AEV_M1, DEV_M1)

        @block.scalar
        def _(act):
            def split(n, c, slot, first_job=None):
                if first_job is not None:
                    act.wait_ge(job_done, first_job)
                act.wait_ge(raw_landed[c], 32 * n + 32)
                nc.scalar.activation(slots[slot][0][:, 2 * c:2 * c + 2, :], raw[:, c], ACT.Copy).then_inc(hi_split, 1)

            def square_sum(norm, t):
                if norm == 0:
                    act.wait_ge(x_landed[t], 16)
                else:
                    act.wait_ge(dev, (DEV_M0, DEV_O, DEV_M1, DEV_END)[norm - 1] - 3 + t)
                if norm >= 1 or t >= 1:
                    act.wait_ge(ss_ready, 4 * norm + t)
                nc.scalar.activation(junk, x[:, t, :], ACT.Square, accum_out=ssum[:, t:t + 1]).then_inc(ss_ready, 1)

            def hT_parts(norm, t):
                for b in range(2):
                    act.wait_ge(xnT_done, 8 * norm + 2 * t + b + 1)
                    nc.scalar.activation(hT[0][:, 4 * b:4 * b + 4, P * t:P * t + P],
                                         bank[4 + 2 * (t % 2) + b][:, :].rearrange("p (k n) -> p k n", k=4),
                                         ACT.Copy).then_inc(hT_hi, 1)

            def norm_tiles(norm):
                for t in range(TT):
                    square_sum(norm, t)
                    if t >= 1 and norm < 4:
                        hT_parts(norm, t - 1)
                if norm < 4:
                    hT_parts(norm, TT - 1)

            square_sum(0, 0)
            split(0, 0, 0)
            square_sum(0, 1)
            hT_parts(0, 0)
            split(0, 1, 0)
            hT_parts(0, 1)
            split(0, 2, 0)
            split(0, 3, 0)
            square_sum(0, 2)
            square_sum(0, 3)
            hT_parts(0, 2)
            hT_parts(0, 3)
            act.wait_ge(wf_landed, 16)
            nc.scalar.activation(wf_split[0][:, :, :], wf[:, :, :], ACT.Copy).then_inc(wf_hi, 1)

            def exps(h, tbs):
                for tb in tbs:
                    c = ORDER.index(tb)
                    act.wait_ge(logit_ready, 4 * h + c + 1)
                    n = P * (tb + 1)
                    v = prob[:, h % 2, OFF[tb]:OFF[tb] + n]
                    pair, k = h // 2, 2 * tb + h % 2
                    nc.scalar.activation(v, v, ACT.Exp, bias=negmax[:, h % 2, c:c + 1], scale=-1.0,
                                         accum_out=den[:, pair % 2, k:k + 1]).then_inc(prob_ready, 1)

            def output_hi(pair):
                act.wait_ge(oT_done, pair + 1)
                nc.scalar.activation(oT[0][:, pair, :], bank[7][:, :], ACT.Copy).then_inc(oT_hi, 1)

            def copy_turned(g, u):
                act.wait_ge(ptT_done, 3 * g + u + 1)
                o, n = OFF[UNITS[u][0]], (512, 512, 256)[u]
                nc.scalar.activation(probT[:, o:o + n], bank[4 + (3 * g + u) % 2][:, 0:n],
                                     ACT.Copy).then_inc(pt_s, 1)

            def step(h, g, v, pair):
                for u in range(3):
                    if h is not None:
                        exps(h, UNITS[u])
                    if g is not None and PT_BY_SCALAR[u]:
                        copy_turned(g, u)
                if pair is not None:
                    output_hi(pair)

            for n, (kind, i) in enumerate(E_PANELS):
                for q in range(4):
                    j = e_first_job(n) + q
                    split(n + 1, q, (n + 1) % 2, e_first_job(n) if q == 0 else None)
                    if kind == "v":
                        act.wait_ge(job_done, j + 1)
                        if i == 0:
                            act.wait_ge(xn_ready, 2)
                        if i == 1:
                            act.wait_ge(pv_done, 8)
                        nc.scalar.activation(v_sb[:, q, :], bank[j % 2][:, :], ACT.Copy).then_inc(aev, 1)
                    if kind == "qk":
                        pair, which = 2 * i + q // 2, q % 2
                        act.wait_ge(job_done, j + 1)
                        if pair >= 2:
                            act.wait_ge(score_done, 6 * (pair - 1))
                        nc.scalar.activation(qk_parts[:, 0, pair % 2, which, :], bank[j % 2][:, :], ACT.Copy,
                                             scale=HD ** -0.5 if which == 0 else 1.0).then_inc(aev, 1)
                    for st in STEPS.get(j, []):
                        step(*st)
                if n == 0:
                    act.wait_ge(gate_abs, 1)
                    nc.scalar.activation(gate[:, 2, :], gate[:, 1, :], ACT.Exp, scale=-1.0).then_inc(gate_exp, 1)
                    act.wait_ge(gate_exp, 1)
                    nc.scalar.activation(gate[:, 1, :], gate[:, 2, :], ACT.Ln, bias=1.0).then_inc(gate_ln, 1)
                if n == 5:
                    for st in TAIL:
                        step(*st)

            def mlp(c, pan, jobs, hids, last=False, first=False):
                for j in range(8):
                    parity = first_bank(jobs, j) if first else (jobs + j) % 2
                    n = 4 * c + j // 4
                    split(pan + n + 1, j % 4, (j // 4 + 1) % 2, jobs + 16 * c + j if j % 4 == 0 else None)
                    act.wait_ge(job_done, jobs + 16 * c + j + 1)
                    nc.scalar.activation(relu_sb[:, j % 2, :], bank[parity][:, :], ACT.Relu).then_inc(aev, 1)
                    act.wait_ge(sq_ready, hids + 8 * c + j + 1)
                    nc.scalar.activation(hid[0][:, j, :], sq_sb[:, j % 2, :], ACT.Copy).then_inc(hid_hi, 1)
                for q in range(8):
                    if not (last and q >= 4):
                        n = 4 * c + 2 + q // 4
                        split(pan + n + 1, q % 4, (q // 4 + 1) % 2, jobs + 16 * c + 8 + q if q % 4 == 0 else None)

            norm_tiles(1)
            mlp(0, PAN_M0, JOB_M0, 0, first=True)
            with act.Fori(1, CHUNKS) as c:
                mlp(c, PAN_M0, JOB_M0, 0)

            norm_tiles(2)

            def r_evac(h, n, s, stage, jobs):
                for q in range(4):
                    split(n + 1, q, 1 - s, jobs if q == 0 else None)
                    act.wait_ge(job_done, jobs + q + 1)
                    src = bank[first_bank(JOB_O, q) if isinstance(h, int) and stage == "qk" else (JOB_O + q) % 2][:, :]
                    if stage == "qk":
                        dst = rq_parts[:, 0, q // 2, q % 2, :]
                    else:
                        dst = (rv_parts[0] if stage == "v" else y_sb)[:, q, :]
                    nc.scalar.activation(dst, src, ACT.Silu if stage == "g" else ACT.Copy).then_inc(aev, 1)

            def r_att_hi(h):
                for s in range(4):
                    o, n = ATT_OFF[s], S - P * s
                    act.wait_ge(att_prod, 4 * h + s + 1)
                    nc.scalar.activation(att_parts[:, 0, o:o + n], att_tmp[:, s % 2, 0:n], ACT.Copy).then_inc(att_hi, 1)

            def r_scale(h):
                for t in range(4):
                    act.wait_ge(gn_r, 4 * h + t + 1)
                    act.wait_ge(y_part, 4 * h + t + 1)
                    nc.scalar.activation(y_sb[:, t, :], y_sb[:, t, :], ACT.Copy,
                                         scale=gn_rstd[:, t:t + 1]).then_inc(y_ready, 1)

            def r_turn(h):
                for k in range(4):
                    act.wait_ge(yT_done, 4 * h + k + 1)
                    nc.scalar.activation(yT[0][:, k, :], bank[2 + k % 2][:, :], ACT.Copy).then_inc(yT_hi, 1)

            def r_out_split(n, s, jobs):
                for c in range(4):
                    split(n + 1, c, 1 - s, jobs if c == 0 else None)

            r_evac(0, PAN_O, 0, "qk", JOB_O)
            r_evac(0, PAN_O + 1, 1, "v", JOB_O + 4)
            r_att_hi(0)
            r_evac(0, PAN_O + 2, 0, "g", JOB_O + 8)
            with act.Fori(1, RH) as h:
                jb = JOB_O - 8 + 20 * h
                r_scale(h - 1)
                r_evac(h, PAN_O - 1 + 4 * h, 1, "qk", jb)
                r_turn(h - 1)
                r_out_split(PAN_O + 4 * h, 0, jb + 4)
                r_evac(h, PAN_O + 1 + 4 * h, 1, "v", jb + 12)
                r_att_hi(h)
                r_evac(h, PAN_O + 2 + 4 * h, 0, "g", jb + 16)
            r_scale(RH - 1)
            r_turn(RH - 1)
            r_out_split(PAN_O + 15, 1, JOB_O + 72)

            norm_tiles(3)
            mlp(0, PAN_M1, JOB_M1, 32, first=True)
            with act.Fori(1, CHUNKS - 1) as c:
                mlp(c, PAN_M1, JOB_M1, 32)
            mlp(CHUNKS - 1, PAN_M1, JOB_M1, 32, last=True)
            norm_tiles(4)

        @block.vector
        def _(dve):
            def split(n, c, slot):
                dve.wait_ge(hi_split, 4 * n + c + 1)
                nc.vector.tensor_tensor(slots[slot][1][:, 2 * c:2 * c + 2, :], raw[:, c],
                                        slots[slot][0][:, 2 * c:2 * c + 2, :].bitcast(F32),
                                        ALU.subtract).then_inc(lo_split, 1)

            def variance(norm, t):
                dve.wait_ge(ss_ready, 4 * norm + t + 1)
                nc.vector.tensor_scalar(var[:, t:t + 1], ssum[:, t:t + 1], 1.0 / D, EPS, ALU.mult,
                                        ALU.add).then_inc(var_ready, 1)

            def normed(norm, t):
                if t == 0:
                    dve.wait_ge(gain_landed, 16 * (norm + 1))
                dve.wait_ge(rstd_ready, 4 * norm + t + 1)
                if norm < 4 and t >= 2:
                    dve.wait_ge(xnT_done, 8 * norm + 2 * (t - 2) + 2)
                if norm == 4 and t >= 2:
                    dve.wait_ge(out_saved[t % 2], 16)
                nc.vector.scalar_tensor_tensor(out=xn[:, t % 2, :], in0=x[:, t, :], scalar=rstd[:, t:t + 1],
                                               in1=gain[:, :], op0=ALU.mult, op1=ALU.mult).then_inc(xn_ready, 1)

            def hT_parts(norm, t):
                for b in range(2):
                    dve.wait_ge(hT_hi, 8 * norm + 2 * t + b + 1)
                    hi = hT[0][:, 4 * b:4 * b + 4, P * t:P * t + P].bitcast(F32)
                    nc.vector.tensor_tensor(hT[1][:, 4 * b:4 * b + 4, P * t:P * t + P],
                                            bank[4 + 2 * (t % 2) + b][:, :].rearrange("p (k n) -> p k n", k=4),
                                            hi, ALU.subtract).then_inc(hT_lo, 1)

            def residual(parity, f, t, jobs_done):
                dve.wait_ge(job_done, jobs_done)
                v = x[:, t, 512 * f:512 * f + 512]
                nc.vector.tensor_tensor(v, bank[parity][:, :], v, ALU.add).then_inc(dev, 1)

            def norm_tiles(norm, last_residual=None):
                for t in range(TT):
                    if last_residual is not None:
                        last_residual(t)
                    variance(norm, t)
                    normed(norm, t)
                    if t >= 1 and norm < 4:
                        hT_parts(norm, t - 1)
                if norm < 4:
                    hT_parts(norm, TT - 1)

            def norm_of(t):
                variance(0, t)
                normed(0, t)

            norm_of(0)
            split(0, 0, 0)
            norm_of(1)
            hT_parts(0, 0)
            split(0, 1, 0)
            hT_parts(0, 1)
            split(0, 2, 0)
            split(0, 3, 0)
            norm_of(2)
            norm_of(3)
            hT_parts(0, 2)
            hT_parts(0, 3)
            dve.wait_ge(ident_landed, 16)
            dve.wait_ge(const_landed, 16 * 4)
            nc.vector.tensor_copy(ident_bf[:, :], ident[:, :]).then_inc(consts_made, 1)
            nc.vector.tensor_copy(causal_bf[:, :], causal).then_inc(consts_made, 1)
            dve.wait_ge(wf_hi, 1)
            nc.vector.tensor_tensor(wf_split[1][:, :, :], wf[:, :, :], wf_split[0][:, :, :].bitcast(F32),
                                    ALU.subtract).then_inc(wf_lo, 1)

            def logits(h, u):
                if h == 0 and u == 0:
                    dve.wait_ge(negc_ready, 1)
                if u == 0:
                    if h < 8:
                        dve.wait_ge(table_ready, h + 1)
                    else:
                        dve.wait_ge(bias_landed[h % 2], 16 * ((h - 8) // 2 + 1))
                if h >= 2 and u == 0:
                    dve.wait_ge(pv_done, h - 1)
                dve.wait_ge(score_done, 3 * h + u + 1)
                col = 0
                for tb in UNITS[u]:
                    n = P * (tb + 1)
                    c = ORDER.index(tb)
                    tab = table[:, h % 2, S - n:S] if h < 8 else table[:, h % 2, 0:n]
                    nc.vector.tensor_tensor_reduce(
                        out=prob[:, h % 2, OFF[tb]:OFF[tb] + n], in0=bank[2 + (3 * h + u) % 2][:, col:col + n],
                        in1=tab, scale=-1.0, scalar=BIG, op0=ALU.add, op1=ALU.min,
                        accum_out=negmax[:, h % 2, c:c + 1]).then_inc(logit_ready, 1)
                    col += n

            def copy_turned(g, u):
                dve.wait_ge(ptT_done, 3 * g + u + 1)
                o, n = OFF[UNITS[u][0]], (512, 512, 256)[u]
                nc.vector.tensor_copy(probT[:, o:o + n], bank[4 + (3 * g + u) % 2][:, 0:n]).then_inc(pt_v, 1)

            def normalise(pair):
                dve.wait_ge(prob_ready, 8 * (pair + 1))
                if pair == 0:
                    dve.wait_ge(negc_saved, 16)
                if pair:
                    dve.wait_ge(oT_done, pair)
                    dve.wait_ge(o_norm, pair)
                nc.vector.reciprocal(rden[:, :], den[:, pair % 2, :]).then_inc(rden_ready, 1)
                dve.wait_ge(rden_ready, pair + 1)
                dve.wait_ge(pv_done, 2 * (pair + 1))
                nc.vector.tensor_tensor(o_sb.rearrange("p (k n) -> p k n", k=8),
                                        bank[6][:, :].rearrange("p (k n) -> p k n", k=8),
                                        rden[:, :].rearrange("p (k o) -> p k o", o=1).to_broadcast([P, 8, HD]),
                                        ALU.mult).then_inc(o_norm, 1)

            def output_lo(pair):
                dve.wait_ge(oT_hi, pair + 1)
                nc.vector.tensor_tensor(oT[1][:, pair, :], bank[7][:, :], oT[0][:, pair, :].bitcast(F32),
                                        ALU.subtract).then_inc(oT_lo, 1)

            def step(h, g, v, pair):
                for u in range(3):
                    if h is not None:
                        logits(h, u)
                    if g is not None and not PT_BY_SCALAR[u]:
                        copy_turned(g, u)
                if v is not None and v % 2 == 1:
                    normalise(v // 2)
                if pair is not None:
                    output_lo(pair)

            for n, (kind, i) in enumerate(E_PANELS):
                for q in range(4):
                    j = e_first_job(n) + q
                    split(n + 1, q, (n + 1) % 2)
                    if kind == "qk":
                        pair, which = 2 * i + q // 2, q % 2
                        dve.wait_ge(aev, e_aev(j))
                        nc.vector.scalar_tensor_tensor(
                            out=qk_parts[:, 1, pair % 2, which, :], in0=bank[j % 2][:, :],
                            scalar=HD ** -0.5 if which == 0 else 1.0,
                            in1=qk_parts[:, 0, pair % 2, which, :].bitcast(F32), op0=ALU.mult,
                            op1=ALU.subtract).then_inc(lev, 1)
                    if kind == "out":
                        if i == 0 and q < 2:
                            dve.wait_ge(x_landed[q], 32)
                        residual(out_bank(j), i, q, j + 1)
                    if kind == "out" and i == 1:
                        variance(1, q)
                        normed(1, q)
                        if q >= 1:
                            hT_parts(1, q - 1)
                    for st in STEPS.get(j, []):
                        step(*st)
                if n == 5:
                    for st in TAIL:
                        step(*st)
                if n == 0:
                    dve.wait_ge(job_done, GATE_JOB + 1)
                    nc.vector.tensor_scalar(gate[:, 0, :], bank[GATE_JOB % 2][0:NFOX, :], bias_f[:, 0:1], None,
                                            ALU.add).then_inc(dev, 1)
                    dve.wait_ge(dev, 1)
                    nc.vector.scalar_tensor_tensor(out=gate[:, 1, :], in0=gate[:, 0, :], scalar=-1.0, in1=gate[:, 0, :],
                                                   op0=ALU.mult, op1=ALU.max).then_inc(gate_abs, 1)
                    nc.vector.tensor_scalar(gate[:, 3, :], gate[:, 0, :], 0.0, None, ALU.min).then_inc(gate_min, 1)
                    dve.wait_ge(gate_min, 1)
                    dve.wait_ge(gate_ln, 1)
                    nc.vector.tensor_tensor_scan(negc, gate[:, 1, :], gate[:, 3, :], 0.0, ALU.add,
                                                 ALU.subtract).then_inc(negc_ready, 1)
            hT_parts(1, TT - 1)

            def mlp(c, pan, jobs, avs, hids, norm=None):
                for j in range(8):
                    split(pan + 4 * c + j // 4 + 1, j % 4, (j // 4 + 1) % 2)
                    dve.wait_ge(hid_lo, hids + 8 * c + j - 1) if (hids or j >= 2 or not isinstance(c, int)) else None
                    dve.wait_ge(aev, avs + 8 * c + j + 1)
                    nc.vector.tensor_tensor(sq_sb[:, j % 2, :], relu_sb[:, j % 2, :], relu_sb[:, j % 2, :],
                                            ALU.mult).then_inc(sq_ready, 1)
                    dve.wait_ge(hid_hi, hids + 8 * c + j + 1)
                    nc.vector.tensor_tensor(hid[1][:, j, :], sq_sb[:, j % 2, :], hid[0][:, j, :].bitcast(F32),
                                            ALU.subtract).then_inc(hid_lo, 1)
                for q in range(8):
                    if not (norm == 4 and q >= 4):
                        split(pan + 4 * c + 3 + q // 4, q % 4, (q // 4 + 1) % 2)
                    residual((jobs + q) % 2, q // 4, q % 4, jobs + 16 * c + 8 + q + 1)
                    if norm is not None and q >= 4:
                        t = q % 4
                        variance(norm, t)
                        normed(norm, t)
                        if t >= 1 and norm < 4:
                            hT_parts(norm, t - 1)
                if norm is not None and norm < 4:
                    hT_parts(norm, TT - 1)

            mlp(0, PAN_M0, JOB_M0, AEV_M0, 0)
            with dve.Fori(1, CHUNKS - 1) as c:
                mlp(c, PAN_M0, JOB_M0, AEV_M0, 0)
            mlp(CHUNKS - 1, PAN_M0, JOB_M0, AEV_M0, 0, norm=2)

            def r_split(n, s):
                for c in range(4):
                    split(n + 1, c, 1 - s)

            def r_lo(h, n, s, stage):
                for q in range(4):
                    split(n + 1, q, 1 - s)
                    src = bank[first_bank(JOB_O, q) if isinstance(h, int) and stage == "qk" else (JOB_O + q) % 2]
                    if stage == "qk":
                        hi, lo = (rq_parts[:, a, q // 2, q % 2, :] for a in range(2))
                    else:
                        hi, lo = (rv_parts[a][:, q, :] for a in range(2))
                    dve.wait_ge(aev, AEV_O + 12 * h + (0 if stage == "qk" else 4) + q + 1)
                    nc.vector.tensor_tensor(lo, src[:, :], hi.bitcast(F32), ALU.subtract).then_inc(lev, 1)

            def r_decay(h, table_row):
                def product(s):
                    n = S - P * s
                    if s >= 2:
                        dve.wait_ge(att_ready, 4 * h + s - 1)
                    dve.wait_ge(rs_done, 4 * h + s + 1)
                    nc.vector.tensor_tensor(att_tmp[:, s % 2, 0:n], bank[2 + s % 2][:, 0:n],
                                            table_row(n), ALU.mult).then_inc(att_prod, 1)

                def low(s):
                    o, n = ATT_OFF[s], S - P * s
                    dve.wait_ge(att_hi, 4 * h + s + 1)
                    nc.vector.tensor_tensor(att_parts[:, 1, o:o + n], att_tmp[:, s % 2, 0:n],
                                            att_parts[:, 0, o:o + n].bitcast(F32), ALU.subtract).then_inc(att_ready, 1)

                product(0)
                for s in range(1, 4):
                    product(s)
                    low(s - 1)
                low(3)

            def r_norm(h):
                def stats(t):
                    nc.vector.bn_stats(gn_stats[:, t, :], bank[4 + t][:, :]).then_inc(gn_st, 1)

                def aggregate(t):
                    nc.vector.bn_aggr(gn_mv[:, t, :], gn_stats[:, t, :]).then_inc(gn_ag, 1)

                dve.wait_ge(ro_done, 4 * h + 1)
                stats(0)
                dve.wait_ge(ro_done, 4 * h + 2)
                dve.wait_ge(gn_st, 4 * h + 1)
                stats(1)
                aggregate(0)
                for t in range(4):
                    dve.wait_ge(gn_ag, 4 * h + t + 1)
                    if t < 2:
                        dve.wait_ge(ro_done, 4 * h + t + 3)
                        dve.wait_ge(gn_st, 4 * h + t + 2)
                        stats(t + 2)
                    if t == 2:
                        dve.wait_ge(gn_st, 4 * h + 4)
                    nc.vector.tensor_scalar(gn_var[:, t:t + 1], gn_mv[:, t, 1:2], EPS, None, ALU.add).then_inc(gn_v, 1)
                    if t < 3:
                        aggregate(t + 1)
                    dve.wait_ge(aev, AEV_O + 12 * h + 8 + t + 1)
                    nc.vector.scalar_tensor_tensor(out=y_sb[:, t, :], in0=bank[4 + t][:, :], scalar=gn_mv[:, t, 0:1],
                                                   in1=y_sb[:, t, :], op0=ALU.subtract,
                                                   op1=ALU.mult).then_inc(y_part, 1)

            def r_turn(h):
                for k in range(4):
                    dve.wait_ge(yT_hi, 4 * h + k + 1)
                    nc.vector.tensor_tensor(yT[1][:, k, :], bank[2 + k % 2][:, :], yT[0][:, k, :].bitcast(F32),
                                            ALU.subtract).then_inc(yT_lo, 1)

            def r_out(n, s, jobs, norm=None):
                for q in range(8):
                    if q % 2 == 0:
                        split(n + 1, q // 2, 1 - s)
                    residual((JOB_O + q) % 2, q // 4, q % 4, jobs + q + 1)
                    if norm is not None and q >= 4:
                        t = q % 4
                        variance(norm, t)
                        normed(norm, t)
                        if t >= 1:
                            hT_parts(norm, t - 1)
                if norm is not None:
                    hT_parts(norm, TT - 1)

            dve.wait_ge(decay_landed, 16)
            r_lo(0, PAN_O, 0, "qk")
            r_lo(0, PAN_O + 1, 1, "v")
            r_decay(0, lambda n: decay[:, 0, 0:n])
            r_split(PAN_O + 2, 0)
            r_norm(0)
            with dve.Fori(1, RH) as h:
                jb = JOB_O - 8 + 20 * h
                r_lo(h, PAN_O - 1 + 4 * h, 1, "qk")
                r_turn(h - 1)
                r_out(PAN_O + 4 * h, 0, jb + 4)
                r_lo(h, PAN_O + 1 + 4 * h, 1, "v")
                r_decay(h, lambda n: decay[:, bass.ds(h, 1), 0:n].rearrange("p a n -> p (a n)"))
                r_split(PAN_O + 2 + 4 * h, 0)
                r_norm(h)
            r_turn(RH - 1)
            r_out(PAN_O + 15, 1, JOB_O + 72, norm=3)

            with dve.Fori(0, CHUNKS - 1) as c:
                mlp(c, PAN_M1, JOB_M1, AEV_M1, 32)
            mlp(CHUNKS - 1, PAN_M1, JOB_M1, AEV_M1, 32, norm=4)

        @block.gpsimd
        def _(pool):
            nc.gpsimd.memset(half_neg[:, :], -0.5).then_inc(half_made, 1)

            def load_gain(norm):
                if norm:
                    pool.wait_ge(xn_ready, 4 * norm)
                pool.dma_start(gain[:, :], gains[norm].to_broadcast([P, D])).then_inc(gain_landed, 16)

            def inv_std(norm):
                for t in range(TT):
                    pool.wait_ge(var_ready, 4 * norm + t + 1)
                    nc.gpsimd.tensor_tensor(rstd[:, t:t + 1], var[:, t:t + 1], half_neg[:, :],
                                            ALU.pow).then_inc(rstd_ready, 1)

            load_gain(0)
            pool.wait_ge(half_made, 1)
            inv_std(0)
            load_gain(1)

            for h in range(8):
                if h == 0:
                    pool.wait_ge(consts_made, 2)
                if h >= 2:
                    pool.wait_ge(logit_ready, 4 * (h - 1))
                nc.gpsimd.tensor_scalar(table[:, h % 2, :], delta, -(2.0 ** -(h + 1)), None,
                                        ALU.mult).then_inc(table_tmp, 1)
                pool.wait_ge(table_tmp, h + 1)
                nc.gpsimd.tensor_tensor(table[:, h % 2, :], table[:, h % 2, :], lncount, ALU.add).then_inc(table_ready, 1)
                if h == 1:
                    pool.wait_ge(negc_ready, 1)
                    pool.dma_start(negc_dram, negc).then_inc(negc_saved, 16)
            pool.wait_ge(negc_saved, 16)
            for h in range(8, 16):
                pool.wait_ge(logit_ready, 4 * (h - 1))
                pool.dma_start(table[:, h % 2, :], negc_dram[h - 8:h - 7, :].to_broadcast([P, S])
                               ).then_inc(bias_landed[h % 2], 16)
            inv_std(1)
            load_gain(2)
            pool.dma_start(decay, c_decay).then_inc(decay_landed, 16)
            inv_std(2)
            load_gain(3)

            def gn_inv_std(h):
                for t in range(4):
                    pool.wait_ge(gn_v, 4 * h + t + 1)
                    nc.gpsimd.tensor_tensor(gn_rstd[:, t:t + 1], gn_var[:, t:t + 1], half_neg[:, :],
                                            ALU.pow).then_inc(gn_r, 1)

            with pool.Fori(0, RH) as h:
                gn_inv_std(h)
            inv_std(3)
            load_gain(4)
            inv_std(4)


_INS = ["x", "norm_mix_g", "norm_ffn_g", "even_w_in", "even_b_f", "even_w_out", "odd_w_in", "odd_w_out",
        "ffn_w_in", "ffn_w_out", "final_g"]


def constants():
    p = np.arange(P)[:, None]
    j = np.arange(S)[None, :]
    eye = np.eye(P, dtype=np.float32)
    causal = np.where(np.arange(P)[None, :] > p, NEG, 0.0).astype(np.float32)
    dist = p + (S - P) - j
    count = (dist >= 0) * ((dist <= 128) * 1 + (dist % 4 == 0) + (dist % 16 == 0))
    lncount = np.where(count > 0, np.log(np.maximum(count, 1)), NEG).astype(np.float32)
    gamma = 1.0 - 2.0 ** (-5.0 - np.arange(RH, dtype=np.float32))
    log_g = np.log(gamma.astype(np.float32)).astype(np.float64)
    rel = j - p
    decay = np.where(rel[:, None, :] >= 0, np.exp(log_g[None, :, None] * np.maximum(rel, 0)[:, None, :]), 0.0) / 16.0
    return {"c_ident": eye, "c_causal": causal, "c_delta": np.maximum(dist, 0).astype(np.float32),
            "c_lncount": lncount, "c_decay": decay.astype(np.float32)}


def kernel(**inputs):
    import concourse.bacc as _bacc
    from concourse.bass_utils import run_bass_kernel_spmd as _run

    nc = _bacc.Bacc("TRN2", target_bir_lowering=False, num_devices=1)
    arrays, args = {}, []
    for name, a in [(n, inputs[n]) for n in _INS] + list(constants().items()):
        a = np.ascontiguousarray(a)
        arrays[f"in_{name}"] = a
        args.append(nc.dram_tensor(f"in_{name}", a.shape, mybir.dt.from_np(a.dtype), kind="ExternalInput").ap())
    args.append(nc.dram_tensor("out_0", (1, S, D), F32, kind="ExternalOutput").ap())
    negc_dram = nc.dram_tensor("negc_dram", (NFOX, S), F32, kind="Internal").ap()
    trunk(nc, *args, negc_dram)
    r = _run(nc, [arrays], core_ids=[0])
    return r.results[0]["out_0"]
```

```python
from contextlib import ExitStack

import numpy as np

import concourse.bass as bass
from concourse import mybir

F32 = mybir.dt.float32
F32R = mybir.dt.float32r
BF16 = mybir.dt.bfloat16
ALU = mybir.AluOpType
ACT = mybir.ActivationFunctionType

P = 128
S = 512
D = 1024
TT = S // P
KT = D // P
HD = 64
WA = 512
NHEAD = 16
NFOX = 8
RH = 4
HID = 4096
CHUNKS = HID // D
EPS = 1e-6
PASSES = ((0, 0), (0, 1), (1, 0))
NEG = -1e30
BIG = 3.0e38

PAN_M0 = 8
PAN_O = PAN_M0 + 4 * CHUNKS
PAN_M1 = PAN_O + 4 * RH
JOB_M0 = 4 * PAN_M0 + 1
JOB_O = JOB_M0 + 16 * CHUNKS
JOB_M1 = JOB_O + 20 * RH
AEV_M0 = 24
AEV_O = AEV_M0 + 8 * CHUNKS
AEV_M1 = AEV_O + 12 * RH
LEV_O = 16
DEV_M0 = 9
DEV_O = DEV_M0 + 8 * CHUNKS
DEV_M1 = DEV_O + 8 * RH
DEV_END = DEV_M1 + 8 * CHUNKS

E_PANELS = [("v", 0), ("qk", 0), ("qk", 1), ("qk", 2), ("v", 1), ("qk", 3), ("out", 0), ("out", 1)]
GATE_JOB = 4
GATE_COLS = 32 + NFOX


def first_bank(jobs, q):
    return 2 + q if q < 2 else (jobs + q) % 2


def e_bank(j):
    return j if j < 4 else j % 2


def e_first_job(n):
    return 4 * n + (1 if n >= 1 else 0)


def e_job_of(pair, which):
    panel = {0: 1, 1: 2, 2: 3, 3: 5}[pair // 2]
    return e_first_job(panel) + 2 * (pair % 2) + which


def e_lev(job):
    return e_aev(job) - (4 if job < e_first_job(4) else 8)


def e_aev(job):
    return job + 1 if job < GATE_JOB else job


STEPS = {7: [(0, None, None, None)],
         8: [(1, 0, None, None)],
         9: [(2, 1, 0, None)],
         10: [(3, 2, 1, None)],
         11: [(4, 3, 2, 0)],
         12: [(5, 4, 3, None)],
         13: [(6, 5, 4, 1)],
         14: [(7, 6, 5, None)],
         15: [(None, 7, 6, 2)],
         16: [(None, None, 7, None)],
         17: [(None, None, None, 3)],
         18: [(8, None, None, None)],
         19: [(9, 8, None, None)],
         21: [(10, 9, 8, None)],
         22: [(11, 10, 9, None)],
         23: [(12, 11, 10, 4)],
         24: [(13, 12, 11, None), (14, 13, 12, 5), (15, 14, 13, None)]}
TAIL = [(None, 15, 14, 6), (None, None, 15, None), (None, None, None, 7)]
EARLY_KT = 6
WARM_UP = 15
PT_BY_SCALAR = (False, False, True)
UNITS = ((3,), (2,), (1, 0))
ORDER = (3, 2, 1, 0)
OFF = {3: 0, 2: 512, 1: 896, 0: 1152}


def pt_count(h, u):
    mine = [v for v in range(3) if PT_BY_SCALAR[v] == PT_BY_SCALAR[u]]
    return PT_BY_SCALAR[u], len(mine) * h + mine.index(u) + 1


def out_bank(j):
    return {27: 2, 28: 3}.get(j, j % 2)


def out_order(at, q):
    return (q % 2, q // 2) if isinstance(at, int) else (q // 4, q % 4)


def trunk(nc, x_in, norm_mix_g, norm_ffn_g, even_w_in, even_b_f, even_w_out, odd_w_in, odd_w_out,
          ffn_w_in, ffn_w_out, final_g, c_ident, c_causal, c_delta, c_lncount, c_decay, out, negc_dram):
    gains = [norm_mix_g[0:1, :], norm_ffn_g[0:1, :], norm_mix_g[1:2, :], norm_ffn_g[1:2, :],
             final_g.rearrange("(a d) -> a d", a=1)]
    x_tiles = x_in.rearrange("b (t p) d -> (b t) p d", p=P)
    out_tiles = out.rearrange("b (t p) d -> (b t) p d", p=P)
    w_even = even_w_in[0]
    w_eout = even_w_out[0]
    w_odd = odd_w_in[0]
    w_oout = odd_w_out[0]

    with ExitStack() as ctx:
        def sb(name, shape, dt=F32):
            return ctx.enter_context(nc.sbuf_tensor(name, shape, dt))

        def sem(name):
            return ctx.enter_context(nc.semaphore(name))

        slots = [[sb(f"w_{part}{s}", [P, 8, 512], F32R) for part in ("hi", "lo")] for s in range(2)]
        raw = sb("raw", [P, 4, 2, 512])
        x_at = nc.sbuf_base
        x = sb("x", [P, TT, D])
        hT = [sb(f"hT_{part}", [P, KT, S], F32R) for part in ("hi", "lo")]
        gain = sb("gain", [P, D])
        arena_at = nc.sbuf_base
        arena = sb("arena", [P, 10752])
        arena_r_at = nc.sbuf_base
        arena_r = sb("arena_r", [P, 16, S], F32R)
        x_q = nc.alloc_sbuf_tensor_at("x_q", [P, TT * D], F32R, offset=x_at)
        arena_q = nc.alloc_sbuf_tensor_at("arena_q", [P, 10752], F32R, offset=arena_at)
        arena_f = nc.alloc_sbuf_tensor_at("arena_f", [P, KT * NFOX], F32, offset=arena_r_at)
        ident = sb("ident", [P, P])
        ident_bf = sb("ident_bf", [P, P], BF16)
        causal_bf = sb("causal_bf", [P, P], BF16)
        bias_f = sb("bias_f", [NFOX, 1])
        negmax = sb("negmax", [P, 2, 4])
        den = sb("den", [P, 2, 8])
        rden = sb("rden", [P, 8])
        ssum = sb("ssum", [P, 4])
        var = sb("var", [P, 4])
        rstd = sb("rstd", [P, 4])
        half_neg = sb("half_neg", [P, 1])
        gn_stats = sb("gn_stats", [P, 4, 6])
        gn_mv = sb("gn_mv", [P, 4, 2])
        gn_var = sb("gn_var", [P, 4])
        gn_rstd = sb("gn_rstd", [P, 4])

        wf = arena_f[:, :].rearrange("p (k n) -> p k n", k=KT)
        wf_stack = arena_q[:, 4096 - GATE_COLS * KT:4096].rearrange("p (k n) -> p k n", k=KT)
        v_sb = x[:, 0:2, :].rearrange("p a (b n) -> p (a b) n", b=2)
        q_stack = arena_q[:, 0:2048].rearrange("p (s h n) -> p s h n", s=2, h=2)
        k_stack = arena_q[:, 2048:4096].rearrange("p (s h n) -> p s h n", s=2, h=2)
        k_lo = x_q[:, 2 * D:3 * D].rearrange("p (s n) -> p s n", s=2)
        ROWS = (slice(0, HD), slice(HD, P))
        prob = arena[:, 4096:6656].rearrange("p (s n) -> p s n", s=2)
        probT = arena[:, 6656:7936]
        table = arena[:, 7936:8960].rearrange("p (s n) -> p s n", s=2)
        delta = arena[:, 8960:9472]
        lncount = arena[:, 9472:9984]
        o_sb = arena[:, 9984:10496]
        gate = arena[0:NFOX, 4096:6144].rearrange("p (s n) -> p s n", s=4)
        negc = o_sb[0:NFOX, :]
        causal = table[:, 0, 0:P]
        zeros = arena[:, 10496:10752].bitcast(BF16)
        xn = arena[:, 4096:6144].rearrange("p (s n) -> p s n", s=2)
        junk = arena[:, 6656:7680]
        relu_sb = arena[:, 0:1024].rearrange("p (s n) -> p s n", s=2)
        sq_sb = arena[:, 1024:2048].rearrange("p (s n) -> p s n", s=2)
        rq_parts = arena_q[:, 0:4096].rearrange("p (a w k n) -> p a w k n", a=2, w=2, k=2)
        att_parts = arena_q[:, 4096:6656].rearrange("p (a n) -> p a n", a=2)
        att_tmp = gain[:, :].rearrange("p (s n) -> p s n", s=2)
        y_sb = arena[:, 6656:8704].rearrange("p (t n) -> p t n", t=TT)
        decay = arena[:, 8704:10752].rearrange("p (h n) -> p h n", h=RH)
        rv_parts = [arena_r[:, 8:12, :], arena_r[:, 12:16, :]]
        ATT_OFF = (0, 512, 896, 1152)
        oT = [arena_r[:, 0:8, :], arena_r[:, 8:16, :]]
        hid = oT
        yT = [arena_r[:, 0:4, :], arena_r[:, 4:8, :]]

        bank = [ctx.enter_context(nc.psum_tensor(f"bank{i}", [P, 512], F32)) for i in range(8)]

        raw_landed = [sem(f"raw_landed{c}") for c in range(4)]
        hi_split = sem("hi_split")
        lo_split = sem("lo_split")
        job_done = sem("job_done")
        aev = sem("aev")
        lev = sem("lev")
        dev = sem("dev")
        x_landed = [sem(f"x_landed{t}") for t in range(TT)]
        ident_landed = sem("ident_landed")
        const_landed = sem("const_landed")
        wf_landed = sem("wf_landed")
        gain_landed = sem("gain_landed")
        decay_landed = sem("decay_landed")
        consts_made = sem("consts_made")
        half_made = sem("half_made")
        half_square = sem("half_square")
        sum_joined = sem("sum_joined")
        zeros_made = sem("zeros_made")
        wf_hi = sem("wf_hi")
        wf_lo = sem("wf_lo")
        ss_ready = sem("ss_ready")
        var_ready = sem("var_ready")
        rstd_ready = sem("rstd_ready")
        xn_ready = sem("xn_ready")
        xnT_done = sem("xnT_done")
        hT_hi = sem("hT_hi")
        hT_lo = sem("hT_lo")
        gate_low = sem("gate_low")
        gate_abs = sem("gate_abs")
        gate_min = sem("gate_min")
        gate_exp = sem("gate_exp")
        gate_ln = sem("gate_ln")
        negc_ready = sem("negc_ready")
        negc_saved = sem("negc_saved")
        table_tmp = sem("table_tmp")
        table_ready = sem("table_ready")
        bias_landed = [sem(f"bias_landed{i}") for i in range(2)]
        score_done = sem("score_done")
        logit_ready = sem("logit_ready")
        prob_ready = sem("prob_ready")
        ptT_done = sem("ptT_done")
        pt_v = sem("pt_v")
        pt_s = sem("pt_s")
        pv_done = sem("pv_done")
        rden_ready = sem("rden_ready")
        o_norm = sem("o_norm")
        oT_done = sem("oT_done")
        oT_hi = sem("oT_hi")
        oT_lo = sem("oT_lo")
        sq_ready = sem("sq_ready")
        hid_hi = sem("hid_hi")
        hid_lo = sem("hid_lo")
        rs_done = sem("rs_done")
        att_prod = sem("att_prod")
        att_hi = sem("att_hi")
        att_ready = sem("att_ready")
        ro_done = sem("ro_done")
        gn_st = sem("gn_st")
        gn_ag = sem("gn_ag")
        gn_v = sem("gn_v")
        gn_r = sem("gn_r")
        y_part = sem("y_part")
        y_ready = sem("y_ready")
        yT_done = sem("yT_done")
        yT_hi = sem("yT_hi")
        yT_lo = sem("yT_lo")
        out_saved = [sem(f"out_saved{i}") for i in range(2)]

        block = ctx.enter_context(nc.Block())

        @block.sync
        def _(sp):
            def load_x(t):
                sp.dma_start(x[:, t, :], x_tiles[t]).then_inc(x_landed[t], 16)

            def quarter(n, c, srcs):
                if not (isinstance(n, int) and n == 0):
                    sp.wait_ge(lo_split, 4 * n + c - 3)
                for e, src in enumerate(srcs):
                    dst = raw[:, c, e, :]
                    if len(src.shape) == 3:
                        dst = dst.rearrange("p (w n) -> p w n", w=2)
                    sp.dma_start(dst, src).then_inc(raw_landed[c], 16)

            def plain(w, r0, c0):
                return [w[bass.ds(r0 + P * k, P), bass.ds(c0, 512)] for k in range(KT)]

            def query_key(w, c0, width):
                return [w[P * k:P * k + P, bass.ds(c0, 2 * width)].rearrange("p (w n) -> p w n", w=2)[:, :, 0:256]
                        for k in range(KT)]

            def panel(n, srcs):
                for c in range(4):
                    quarter(n, c, srcs[2 * c:2 * c + 2])

            def e_panel(n):
                kind, i = E_PANELS[n]
                if kind == "v":
                    return plain(w_even, 0, 3 * WA * i + 2 * WA)
                if kind == "qk":
                    return query_key(w_even, 3 * WA * (i // 2) + 256 * (i % 2), WA)
                return plain(w_eout, 0, 512 * i)

            load_x(0)
            sp.dma_start(ident[:, :], c_ident).then_inc(ident_landed, 16)
            first = e_panel(0)
            quarter(0, 0, first[0:2])
            quarter(0, 1, first[2:4])
            load_x(1)
            for c in range(2, 4):
                quarter(0, c, first[2 * c:2 * c + 2])
            load_x(2)
            load_x(3)
            with nc.allow_non_contiguous_dma(reason="eight biases, one a partition"):
                for dst, src in ((causal, c_causal), (delta, c_delta), (lncount, c_lncount),
                                 (bias_f[:, :], even_b_f.rearrange("a f -> f a"))):
                    sp.dma_start(dst, src).then_inc(const_landed, 16)
            sp.dma_start(wf[:, :, :], w_even[:, 6 * WA:6 * WA + NFOX].rearrange("(k p) n -> p k n", p=P)
                         ).then_inc(wf_landed, 16)
            for n in range(1, PAN_M0):
                panel(n, e_panel(n))
            sp.wait_ge(pv_done, NHEAD)
            for t in range(3):
                load_x(t)

            def mlp(layer, base, c):
                w1, w2 = ffn_w_in[layer], ffn_w_out[layer]
                for e in range(2):
                    panel(base + 4 * c + e, plain(w1, 0, 1024 * c + 512 * e))
                for e in range(2):
                    panel(base + 4 * c + 2 + e, plain(w2, 1024 * c, 512 * e))

            with sp.Fori(0, CHUNKS) as c:
                mlp(0, PAN_M0, c)

            def head_qk(h):
                v = w_odd[:, 0:2 * D].rearrange("r (w n) -> r w n", w=2)
                return [v[P * k:P * k + P, :, bass.ds(256 * h, 256)] for k in range(KT)]

            def head_out(h):
                return [w_oout[bass.ds(512 * h + P * c, P), 512 * f:512 * f + 512] for c in range(4) for f in range(2)]

            panel(PAN_O, head_qk(0))
            panel(PAN_O + 1, plain(w_odd, 0, 2 * D))
            panel(PAN_O + 2, plain(w_odd, 0, 4 * D))
            with sp.Fori(1, RH) as h:
                panel(PAN_O - 1 + 4 * h, head_qk(h))
                panel(PAN_O + 4 * h, plain(w_odd, 0, 2 * D + 512 * h))
                panel(PAN_O + 1 + 4 * h, plain(w_odd, 0, 4 * D + 512 * h))
                panel(PAN_O + 2 + 4 * h, head_out(h - 1))
            panel(PAN_O + 15, head_out(RH - 1))
            with sp.Fori(0, CHUNKS) as c:
                mlp(1, PAN_M1, c)
            for t in range(TT - 1):
                sp.wait_ge(xn_ready, 16 + t + 1)
                sp.dma_start(out_tiles[t], xn[:, t % 2, :]).then_inc(out_saved[t % 2], 16)
            for f in range(2):
                half = slice(512 * f, 512 * f + 512)
                sp.wait_ge(xn_ready, 16 + TT + f)
                sp.dma_start(out_tiles[TT - 1][:, half], xn[:, 1, half]).then_inc(out_saved[1], 16)
            sp.wait_ge(out_saved[0], 16 * 2)
            sp.wait_ge(out_saved[1], 16 * 3)

        @block.tensor
        def _(pe):
            def job(parity, stat, mov, slot_waits, kts=KT, first=None):
                for k in range(kts):
                    slot_waits(k)
                    for n, (a, b) in enumerate(PASSES):
                        mm = pe.matmul(bank[parity][:, :] if first is None else bank[parity][0:first, :],
                                       stat(k, a), mov(k, b),
                                       start=(k == 0 and n == 0), stop=(k == kts - 1 and n == 2))
                mm.then_inc(job_done, 1)

            def nowait(k):
                pass

            def quarter_wait(n):
                def w(k):
                    if k % 2 == 0:
                        pe.wait_ge(lo_split, 4 * n + k // 2 + 1)
                return w

            def turn_xn(norm, t):
                pe.wait_ge(xn_ready, 4 * norm + t + 1)
                for b in range(2):
                    if t >= 2:
                        pe.wait_ge(hT_lo, 8 * norm + 2 * (t - 2) + b + 1)
                    dst = bank[4 + 2 * (t % 2) + b]
                    for k in range(4):
                        mm = pe.transpose(dst[:, P * k:P * k + P],
                                          xn[:, t % 2, P * (4 * b + k):P * (4 * b + k) + P], ident[:, :])
                    mm.then_inc(xnT_done, 1)

            def first_panel(norm, n, slot):
                w = slots[slot]
                jobs, devs = {1: (JOB_M0, DEV_M0), 2: (JOB_O, DEV_O), 3: (JOB_M1, DEV_M1)}[norm]
                turn_xn(norm, 2)
                for half in range(2):
                    pe.wait_ge(hT_lo, 8 * norm + 4 * half + 4)
                    for q in range(4):
                        if half == 0 and q == 2:
                            turn_xn(norm, 3)
                            pe.wait_ge(dev, devs)
                        dst = bank[first_bank(jobs, q)]
                        c = 256 * half
                        for k in range(KT):
                            if half == 0 and q == 0 and k % 2 == 0:
                                pe.wait_ge(lo_split, 4 * n + k // 2 + 1)
                            for i, (a, b) in enumerate(PASSES):
                                mm = pe.matmul(dst[:, c:c + 256], w[a][:, k, P * q:P * q + P],
                                               hT[b][:, k, c:c + 256],
                                               start=(k == 0 and i == 0), stop=(k == KT - 1 and i == 2))
                        if half == 1:
                            mm.then_inc(job_done, 1)

            def keep_busy(count):
                for _ in range(count):
                    pe.matmul(bank[3][:, :], zeros[:, 0:P], zeros, start=True, stop=True)

            pe.wait_ge(zeros_made, 1)
            keep_busy(WARM_UP)
            pe.wait_ge(ident_landed, 16)

            def scores_unit(h, u):
                q = 3 * h + u
                ready = ((4 * h - 1), 4 * h, 4 * h + 1)[u]
                if ready > 0:
                    pe.wait_ge(logit_ready, ready)
                if u == 0:
                    pe.wait_ge(lev, e_lev(e_job_of(h // 2, 1)))
                dst = bank[2 + q % 2]
                col = 0
                own, head, st = ROWS[h % 2], h % 2, (h // 2) % 2
                fox = h >= 8
                if h == 8 and u == 0:
                    pe.wait_ge(consts_made, 2)
                for tb in UNITS[u]:
                    n = P * (tb + 1)
                    tokens = slice(P * tb, P * tb + P)
                    pe.matmul(dst[:, col:col + n], q_stack[:, st, head, tokens], k_stack[:, st, head, 0:n],
                              start=True, stop=False)
                    mm = pe.matmul(dst[:, col:col + n], q_stack[own, st, head, tokens], k_lo[own, st, 0:n],
                                   start=False, stop=not fox)
                    if fox:
                        mm = pe.matmul(dst[:, col + n - P:col + n], ident_bf[:, :], causal_bf[:, :],
                                       start=False, stop=True)
                    col += n
                mm.then_inc(score_done, 1)

            def pt_wait(h, u):
                by_scalar, count = pt_count(h, u)
                pe.wait_ge(pt_s if by_scalar else pt_v, count)

            def turn_prob(h, u):
                q = 3 * h + u
                pe.wait_ge(prob_ready, 4 * h + (1, 2, 4)[u])
                if q >= 2:
                    pt_wait((q - 2) // 3, (q - 2) % 3)
                dst = bank[4 + q % 2]
                col = 0
                for tb in UNITS[u]:
                    for s in range(tb + 1):
                        mm = pe.transpose(dst[:, col:col + P], prob[:, h % 2, OFF[tb] + P * s:OFF[tb] + P * s + P],
                                          ident[:, :])
                        col += P
                mm.then_inc(ptT_done, 1)

            def gather_values(h):
                if h % 2 == 0 and h >= 2:
                    pe.wait_ge(o_norm, h // 2)
                pe.wait_ge(aev, e_aev(e_first_job(0 if h < 8 else 4) + 3))
                for u in range(3):
                    pt_wait(h, u)
                    for tb in UNITS[u]:
                        for s in range(tb + 1):
                            c = P * tb + HD * (h % 2)
                            o = OFF[tb] + P * s
                            mm = pe.matmul(bank[6][:, c:c + HD], probT[:, o:o + P],
                                           v_sb[:, s, HD * (h % 8):HD * (h % 8) + HD],
                                           start=(s == 0), stop=(s == tb))
                mm.then_inc(pv_done, 1)

            def turn_output(pair):
                pe.wait_ge(o_norm, pair + 1)
                if pair:
                    pe.wait_ge(oT_lo, pair)
                for t in range(TT):
                    mm = pe.transpose(bank[7][:, P * t:P * t + P], o_sb[:, P * t:P * t + P], ident[:, :])
                mm.then_inc(oT_done, 1)

            def out_part(j, ks):
                n = 6 + (j - e_first_job(6)) // 4
                w, t = slots[n % 2], (j - e_first_job(6)) % 4
                for k in ks:
                    if t == 0 and k % 2 == 0:
                        pe.wait_ge(lo_split, 4 * n + k // 2 + 1)
                    if j == e_first_job(6):
                        pe.wait_ge(oT_lo, k + 1)
                    for i, (a, b) in enumerate(PASSES):
                        mm = pe.matmul(bank[out_bank(j)][:, :], oT[a][:, k, P * t:P * t + P], w[b][:, k, :],
                                       start=(k == 0 and i == 0), stop=(k == KT - 1 and i == 2))
                if ks[-1] == KT - 1:
                    mm.then_inc(job_done, 1)

            def e_job_free(j):
                if j < 2:
                    return
                p = {29: 25, 30: 26}.get(j, j - 2)
                if p == GATE_JOB:
                    pe.wait_ge(dev, 1)
                elif p < 4 or 17 <= p < 21:
                    pe.wait_ge(aev, e_aev(p))
                elif p < 25:
                    pe.wait_ge(lev, e_lev(p))
                else:
                    pe.wait_ge(dev, 1 + p - 24)

            def value_part(q, c):
                pe.wait_ge(lo_split, c + 1)
                pe.wait_ge(hT_lo, 2 * q + 1 + c // 2)
                w = slots[0]
                for k in (2 * c, 2 * c + 1):
                    for i, (a, b) in enumerate(PASSES):
                        mm = pe.matmul(bank[e_bank(q)][:, :], hT[a][:, k, P * q:P * q + P], w[b][:, k, :],
                                       start=(k == 0 and i == 0), stop=(k == KT - 1 and i == 2))
                if c == 3:
                    mm.then_inc(job_done, 1)

            turn_xn(0, 0)
            keep_busy(WARM_UP // 2)
            value_part(0, 0)
            value_part(0, 1)
            turn_xn(0, 1)
            for q, c in ((0, 2), (1, 0), (1, 1), (1, 2), (0, 3), (1, 3)):
                value_part(q, c)
            turn_xn(0, 2)
            turn_xn(0, 3)
            for q in (2, 3):
                for c in range(4):
                    value_part(q, c)

            def project(j, k, stat, mov):
                if k == 0:
                    e_job_free(j)
                for i, (a, b) in enumerate(PASSES):
                    mm = pe.matmul(bank[e_bank(j)][:, :], stat(k, a), mov(k, b), start=(k == 0 and i == 0),
                                   stop=(k == KT - 1 and i == 2))
                if k == KT - 1:
                    mm.then_inc(job_done, 1)

            pe.wait_ge(wf_lo, 1)
            e_job_free(GATE_JOB)
            for k in range(KT):
                mm = pe.matmul(bank[GATE_JOB % 2][0:GATE_COLS, :], wf_stack[:, k, :], hT[0][:, k, :],
                               start=(k == 0), stop=(k == KT - 1))
                if k < KT - 1:
                    for kk in (k, KT - 1) if k == 0 else (k,):
                        pe.matmul(bank[GATE_JOB % 2][0:NFOX, :], wf_stack[:, kk, 0:NFOX], hT[1][:, kk, :],
                                  start=False, stop=False)
            mm.then_inc(job_done, 1)

            def k_tile(j, k):
                n = (j - 1) // 4
                q, w = j - e_first_job(n), slots[n % 2]
                if n >= 6:
                    if k == 0 and j < 27:
                        e_job_free(j)
                    if k == 0 and j == 27:
                        pe.wait_ge(logit_ready, 4 * NHEAD)
                    out_part(j, [k])
                    return
                if q == 0 and k % 2 == 0:
                    pe.wait_ge(lo_split, 4 * n + k // 2 + 1)
                if E_PANELS[n][0] == "v":
                    project(j, k, lambda k, a: hT[a][:, k, P * q:P * q + P], lambda k, b: w[b][:, k, :])
                else:
                    c = 256 * (q % 2) + P * (q // 2)
                    project(j, k, lambda k, a: w[a][:, k, c:c + P], lambda k, b: hT[b][:, k, :])

            def attention(h, g, v, pair, n):
                u, what = n // 3, n % 3
                if n == 9:
                    if pair is not None:
                        turn_output(pair)
                elif what == 0 and h is not None:
                    scores_unit(h, u)
                elif what == 1 and u == 0 and v is not None:
                    gather_values(v)
                elif what == 2 and g is not None:
                    turn_prob(g, u)

            def beside(steps, jobs_k):
                pieces = 10 * len(steps)
                for i, (j, k) in enumerate(jobs_k):
                    k_tile(j, k)
                    for n in range(i * pieces // len(jobs_k), (i + 1) * pieces // len(jobs_k)):
                        attention(*steps[n // 10], n % 10)

            for j in range(GATE_JOB + 1, 25):
                beside(STEPS.get(j - 1, []), [(j, k) for k in range(KT)])

            last = STEPS[24]
            beside(last[0:1], [(25, 0), (25, 1), (25, 2)])
            beside(last[1:2], [(25, 3), (25, 4), (26, 0), (26, 1), (26, 2), (26, 3)])
            beside(last[2:3], [(26, 4), (25, 5)])
            beside(TAIL[0:1], [(26, 5), (27, 0), (27, 1), (27, 2), (27, 3), (27, 4)])
            beside(TAIL[1:2], [(27, 5), (28, 0), (28, 1)])
            beside(TAIL[2:3], [(28, 2), (28, 3)])
            beside([], [(28, 4), (28, 5)])
            for j in range(25, 29):
                out_part(j, range(EARLY_KT, KT))
            for j in range(29, 33):
                e_job_free(j)
                out_part(j, range(KT))
                if j in (30, 31):
                    turn_xn(1, j - 30)

            def mlp(c, pan, jobs, avs, dvs, first=None, last=None):
                if first is not None:
                    first_panel(first, pan, 0)
                for j in range(0 if first is None else 4, 8):
                    w = slots[j // 4]
                    if j < 2:
                        pe.wait_ge(dev, dvs + 8 * c - 1 + j)
                    else:
                        pe.wait_ge(aev, avs + 8 * c + j - 1)
                    waits = quarter_wait(pan + 4 * c + j // 4) if j % 4 == 0 else nowait
                    col = P * (j % 4)
                    job((jobs + j) % 2, lambda k, a: w[a][:, k, col:col + P], lambda k, b: hT[b][:, k, :], waits)
                for q in range(8):
                    w = slots[q // 4]
                    if q < 2:
                        pe.wait_ge(aev, avs + 8 * c + 7 + q)
                    else:
                        pe.wait_ge(dev, dvs + 8 * c + q - 1)
                    waits = quarter_wait(pan + 4 * c + 2 + q // 4) if q % 4 == 0 else nowait

                    def both(k, waits=waits, q=q):
                        waits(k)
                        if q == 0:
                            pe.wait_ge(hid_lo, (avs_hid[jobs]) + 8 * c + k + 1)
                    t = q % 4
                    job((jobs + q) % 2, lambda k, a: hid[a][:, k, P * t:P * t + P], lambda k, b: w[b][:, k, :], both)
                    if last is not None and q in (5, 6):
                        turn_xn(last, q - 5)

            avs_hid = {JOB_M0: 0, JOB_M1: 32}
            mlp(0, PAN_M0, JOB_M0, AEV_M0, DEV_M0, first=1)
            with pe.Fori(1, CHUNKS - 1) as c:
                mlp(c, PAN_M0, JOB_M0, AEV_M0, DEV_M0)
            mlp(CHUNKS - 1, PAN_M0, JOB_M0, AEV_M0, DEV_M0, last=2)


            def r_free(h, stage, q):
                if stage == "qk":
                    if q < 2:
                        pe.wait_ge(aev, AEV_O + 12 * h - 1 + q)
                        pe.wait_ge(dev, DEV_O + 8 * (h - 2) + 7 + q)
                    else:
                        pe.wait_ge(lev, LEV_O + 8 * h + q - 1)
                elif stage == "v":
                    pe.wait_ge(lev, LEV_O + 8 * h + 3 + q)
                elif stage == "g":
                    if q < 2:
                        pe.wait_ge(lev, LEV_O + 8 * h + 7 + q)
                    else:
                        pe.wait_ge(aev, AEV_O + 12 * h + 7 + q)
                elif q >= 2:
                    pe.wait_ge(dev, DEV_O + 8 * (h - 1) + q - 1)
                elif isinstance(h, int) and h == RH:
                    pe.wait_ge(dev, DEV_O + 8 * (h - 2) + 7 + q)
                else:
                    pe.wait_ge(aev, AEV_O + 12 * h + 11 + q)

            def r_qk(h, n, s):
                w = slots[s]
                for q in range(4):
                    r_free(h, "qk", q)
                    job((JOB_O + q) % 2, lambda k, a: w[a][:, k, P * q:P * q + P], lambda k, b: hT[b][:, k, :],
                        quarter_wait(n) if q == 0 else nowait)

            def r_vg(h, n, s, stage):
                w = slots[s]
                for q in range(4):
                    r_free(h, stage, q)
                    job((JOB_O + q) % 2, lambda k, a: hT[a][:, k, P * q:P * q + P], lambda k, b: w[b][:, k, :],
                        quarter_wait(n) if q == 0 else nowait)

            def r_scores(h):
                for s in range(4):
                    if s == 0:
                        pe.wait_ge(lev, LEV_O + 8 * h + 4)
                    if s >= 2:
                        pe.wait_ge(att_prod, 4 * h + s - 1)
                    n = S - P * s
                    for k in range(2):
                        for i, (a, b) in enumerate(PASSES):
                            mm = pe.matmul(bank[2 + s % 2][:, 0:n], rq_parts[:, a, 1, k, P * s:P * s + P],
                                           rq_parts[:, b, 0, k, S - n:S],
                                           start=(k == 0 and i == 0), stop=(k == 1 and i == 2))
                    mm.then_inc(rs_done, 1)

            def r_values(h):
                pe.wait_ge(lev, LEV_O + 8 * h + 8)
                for t in range(4):
                    pe.wait_ge(att_ready, 4 * h + t + 1)
                    if not (isinstance(h, int) and h == 0):
                        pe.wait_ge(yT_lo, 4 * h - 3 + t)
                    for s in range(t + 1):
                        o = ATT_OFF[s] + P * (t - s)
                        for i, (a, b) in enumerate(PASSES):
                            mm = pe.matmul(bank[4 + t][:, :], att_parts[:, a, o:o + P], rv_parts[b][:, s, :],
                                           start=(s == 0 and i == 0), stop=(s == t and i == 2))
                    mm.then_inc(ro_done, 1)

            def r_turn(h):
                for k in range(4):
                    for t in range(4):
                        if k == 0:
                            pe.wait_ge(y_ready, 4 * h + t + 1)
                        mm = pe.transpose(bank[4 + k][:, P * t:P * t + P], y_sb[:, t, P * k:P * k + P], ident[:, :])
                    mm.then_inc(yT_done, 1)

            def r_out(h, n, s, at):
                w = [slots[s][b][:, :, :].rearrange("p (k f) n -> p k (f n)", f=2) for b in range(2)]
                for q in range(8):
                    r_free(at, "out", q)
                    f, t = out_order(at, q)

                    def waits(k, q=q):
                        if q == 0:
                            pe.wait_ge(lo_split, 4 * n + k + 1)
                            pe.wait_ge(yT_lo, 4 * h + k + 1)
                    job((JOB_O + q) % 2, lambda k, a: yT[a][:, k, P * t:P * t + P],
                        lambda k, b: w[b][:, k, 512 * f:512 * f + 512], waits, kts=4)
                    if isinstance(at, int) and q in (4, 6):
                        turn_xn(3, (q - 4) // 2)

            first_panel(2, PAN_O, 0)
            r_vg(0, PAN_O + 1, 1, "v")
            r_scores(0)
            r_vg(0, PAN_O + 2, 0, "g")
            r_values(0)
            with pe.Fori(1, RH) as h:
                r_qk(h, PAN_O - 1 + 4 * h, 1)
                r_turn(h - 1)
                r_vg(h, PAN_O + 4 * h, 0, "v")
                r_scores(h)
                r_vg(h, PAN_O + 1 + 4 * h, 1, "g")
                r_values(h)
                r_out(h - 1, PAN_O + 2 + 4 * h, 0, h)
            r_turn(RH - 1)
            r_out(RH - 1, PAN_O + 15, 1, RH)

            mlp(0, PAN_M1, JOB_M1, AEV_M1, DEV_M1, first=3)
            with pe.Fori(1, CHUNKS) as c:
                mlp(c, PAN_M1, JOB_M1, AEV_M1, DEV_M1)

        @block.scalar
        def _(act):
            def split(n, c, slot, first_job=None):
                if first_job is not None:
                    act.wait_ge(job_done, first_job)
                act.wait_ge(raw_landed[c], 32 * n + 32)
                nc.scalar.activation(slots[slot][0][:, 2 * c:2 * c + 2, :], raw[:, c], ACT.Copy).then_inc(hi_split, 1)

            def square_sum(norm, t):
                if norm == 0:
                    act.wait_ge(x_landed[t], 16)
                else:
                    act.wait_ge(dev, (DEV_M0, DEV_O, DEV_M1, DEV_END)[norm - 1] - (6 - 2 * t if norm == 3 else 3 - t))
                if norm >= 1 or t >= 1:
                    act.wait_ge(ss_ready, 4 * norm + t)
                if norm == 4 and t == TT - 1:
                    act.wait_ge(half_square, 1)
                    nc.scalar.activation(junk[:, 512:D], x[:, t, 512:D], ACT.Square,
                                         accum_out=ssum[:, t:t + 1]).then_inc(ss_ready, 1)
                    return
                nc.scalar.activation(junk, x[:, t, :], ACT.Square, accum_out=ssum[:, t:t + 1]).then_inc(ss_ready, 1)

            def hT_parts(norm, t):
                for b in range(2):
                    act.wait_ge(xnT_done, 8 * norm + 2 * t + b + 1)
                    nc.scalar.activation(hT[0][:, 4 * b:4 * b + 4, P * t:P * t + P],
                                         bank[4 + 2 * (t % 2) + b][:, :].rearrange("p (k n) -> p k n", k=4),
                                         ACT.Copy).then_inc(hT_hi, 1)

            def norm_tiles(norm):
                for t in range(TT):
                    if norm == 4 and t == TT - 1:
                        act.wait_ge(ss_ready, 4 * norm + t)
                        act.wait_ge(var_ready, 4 * norm + 1)
                        nc.scalar.activation(junk[:, 0:512], x[:, t, 0:512], ACT.Square,
                                             accum_out=ssum[:, 0:1]).then_inc(half_square, 1)
                    square_sum(norm, t)
                    if norm == 1 and t < 2:
                        split(PAN_M0, 2 + t, 0)
                    if t >= 1 and norm < 4:
                        hT_parts(norm, t - 1)
                if norm < 4:
                    hT_parts(norm, TT - 1)

            square_sum(0, 0)
            split(0, 0, 0)
            hT_parts(0, 0)
            split(0, 1, 0)
            square_sum(0, 1)
            split(0, 2, 0)
            hT_parts(0, 1)
            split(0, 3, 0)
            square_sum(0, 2)
            square_sum(0, 3)
            hT_parts(0, 2)
            hT_parts(0, 3)
            act.wait_ge(wf_landed, 16)
            nc.scalar.activation(wf_stack[:, :, 0:32].rearrange("p k (a n) -> p k a n", a=4),
                                 wf.rearrange("p k (a n) -> p k a n", a=1).to_broadcast([P, KT, 4, NFOX]),
                                 ACT.Copy).then_inc(wf_hi, 1)

            def exps(h, tbs):
                for tb in tbs:
                    c = ORDER.index(tb)
                    act.wait_ge(logit_ready, 4 * h + c + 1)
                    n = P * (tb + 1)
                    v = prob[:, h % 2, OFF[tb]:OFF[tb] + n]
                    pair, k = h // 2, 2 * tb + h % 2
                    nc.scalar.activation(v, v, ACT.Exp, bias=negmax[:, h % 2, c:c + 1], scale=-1.0,
                                         accum_out=den[:, pair % 2, k:k + 1]).then_inc(prob_ready, 1)

            def output_hi(pair):
                act.wait_ge(oT_done, pair + 1)
                nc.scalar.activation(oT[0][:, pair, :], bank[7][:, :], ACT.Copy).then_inc(oT_hi, 1)

            def copy_turned(g, u):
                act.wait_ge(ptT_done, 3 * g + u + 1)
                o, n = OFF[UNITS[u][0]], (512, 384, 384)[u]
                nc.scalar.activation(probT[:, o:o + n], bank[4 + (3 * g + u) % 2][:, 0:n],
                                     ACT.Copy).then_inc(pt_s, 1)

            def step(h, g, v, pair):
                for u in range(3):
                    if h is not None:
                        exps(h, UNITS[u])
                    if g is not None and PT_BY_SCALAR[u]:
                        copy_turned(g, u)
                if pair is not None:
                    output_hi(pair)

            for n, (kind, i) in enumerate(E_PANELS):
                for q in range(4):
                    j = e_first_job(n) + q
                    if not (n == 7 and q >= 2):
                        split(n + 1, q, (n + 1) % 2, e_first_job(n) if q == 0 else None)
                    if kind == "v":
                        act.wait_ge(job_done, j + 1)
                        if i == 0:
                            act.wait_ge(xn_ready, 2)
                        if i == 1:
                            act.wait_ge(pv_done, 8)
                        nc.scalar.activation(v_sb[:, q, :], bank[e_bank(j)][:, :], ACT.Copy).then_inc(aev, 1)
                    if kind == "qk":
                        pair, which = 2 * i + q // 2, q % 2
                        act.wait_ge(job_done, j + 1)
                        if pair >= 2:
                            act.wait_ge(score_done, 6 * (pair - 1))
                        st, src = pair % 2, bank[j % 2]
                        for head, own in enumerate(ROWS):
                            if which == 0:
                                last = nc.scalar.activation(q_stack[own, st, head, :], src[own, :], ACT.Copy,
                                                            scale=HD ** -0.5)
                            else:
                                for rows in ROWS:
                                    last = nc.scalar.activation(k_stack[rows, st, head, :], src[own, :], ACT.Copy)
                        last.then_inc(aev, 1)
                    for st in STEPS.get(j, []):
                        step(*st)
                if n == 0:
                    act.wait_ge(job_done, GATE_JOB + 1)
                    nc.scalar.activation(gate[:, 2, :], bank[GATE_JOB % 2][32:GATE_COLS, :], ACT.Copy
                                         ).then_inc(gate_low, 1)
                    act.wait_ge(gate_abs, 1)
                    nc.scalar.activation(gate[:, 2, :], gate[:, 1, :], ACT.Exp, scale=-1.0).then_inc(gate_exp, 1)
                    act.wait_ge(gate_exp, 1)
                    nc.scalar.activation(gate[:, 1, :], gate[:, 2, :], ACT.Ln, bias=1.0).then_inc(gate_ln, 1)
                if n == 5:
                    for st in TAIL:
                        step(*st)

            def mlp(c, pan, jobs, hids, last=False, first=False):
                for j in range(8):
                    parity = first_bank(jobs, j) if first else (jobs + j) % 2
                    n = 4 * c + j // 4
                    split(pan + n + 1, j % 4, (j // 4 + 1) % 2, jobs + 16 * c + j if j % 4 == 0 else None)
                    act.wait_ge(job_done, jobs + 16 * c + j + 1)
                    nc.scalar.activation(relu_sb[:, j % 2, :], bank[parity][:, :], ACT.Relu).then_inc(aev, 1)
                    act.wait_ge(sq_ready, hids + 8 * c + j + 1)
                    nc.scalar.activation(hid[0][:, j, :], sq_sb[:, j % 2, :], ACT.Copy).then_inc(hid_hi, 1)
                for q in range(8):
                    if not (last and q >= 4):
                        n = 4 * c + 2 + q // 4
                        split(pan + n + 1, q % 4, (q // 4 + 1) % 2, jobs + 16 * c + 8 + q if q % 4 == 0 else None)

            norm_tiles(1)
            mlp(0, PAN_M0, JOB_M0, 0, first=True)
            with act.Fori(1, CHUNKS) as c:
                mlp(c, PAN_M0, JOB_M0, 0)

            norm_tiles(2)

            def r_evac(h, n, s, stage, jobs):
                for q in range(4):
                    split(n + 1, q, 1 - s, jobs if q == 0 else None)
                    act.wait_ge(job_done, jobs + q + 1)
                    src = bank[first_bank(JOB_O, q) if isinstance(h, int) and stage == "qk" else (JOB_O + q) % 2][:, :]
                    if stage == "qk":
                        dst = rq_parts[:, 0, q // 2, q % 2, :]
                    else:
                        dst = (rv_parts[0] if stage == "v" else y_sb)[:, q, :]
                    nc.scalar.activation(dst, src, ACT.Silu if stage == "g" else ACT.Copy).then_inc(aev, 1)

            def r_att_hi(h):
                for s in range(4):
                    o, n = ATT_OFF[s], S - P * s
                    act.wait_ge(att_prod, 4 * h + s + 1)
                    nc.scalar.activation(att_parts[:, 0, o:o + n], att_tmp[:, s % 2, 0:n], ACT.Copy).then_inc(att_hi, 1)

            def r_scale(h):
                for t in range(4):
                    act.wait_ge(gn_r, 4 * h + t + 1)
                    act.wait_ge(y_part, 4 * h + t + 1)
                    nc.scalar.activation(y_sb[:, t, :], y_sb[:, t, :], ACT.Copy,
                                         scale=gn_rstd[:, t:t + 1]).then_inc(y_ready, 1)

            def r_turn(h):
                for k in range(4):
                    act.wait_ge(yT_done, 4 * h + k + 1)
                    nc.scalar.activation(yT[0][:, k, :], bank[4 + k][:, :], ACT.Copy).then_inc(yT_hi, 1)

            def r_out_split(n, s, jobs):
                for c in range(4):
                    split(n + 1, c, 1 - s, jobs if c == 0 else None)

            r_evac(0, PAN_O, 0, "qk", JOB_O)
            r_evac(0, PAN_O + 1, 1, "v", JOB_O + 4)
            r_att_hi(0)
            r_evac(0, PAN_O + 2, 0, "g", JOB_O + 8)
            r_scale(0)
            with act.Fori(1, RH) as h:
                jb = JOB_O - 8 + 20 * h
                r_evac(h, PAN_O - 1 + 4 * h, 1, "qk", jb)
                r_turn(h - 1)
                r_evac(h, PAN_O + 4 * h, 0, "v", jb + 4)
                r_att_hi(h)
                r_evac(h, PAN_O + 1 + 4 * h, 1, "g", jb + 8)
                r_scale(h)
                r_out_split(PAN_O + 2 + 4 * h, 0, jb + 12)
            r_turn(RH - 1)
            r_out_split(PAN_O + 15, 1, JOB_O + 72)

            norm_tiles(3)
            mlp(0, PAN_M1, JOB_M1, 32, first=True)
            with act.Fori(1, CHUNKS - 1) as c:
                mlp(c, PAN_M1, JOB_M1, 32)
            mlp(CHUNKS - 1, PAN_M1, JOB_M1, 32, last=True)
            norm_tiles(4)

        @block.vector
        def _(dve):
            def split(n, c, slot):
                dve.wait_ge(hi_split, 4 * n + c + 1)
                nc.vector.tensor_tensor(slots[slot][1][:, 2 * c:2 * c + 2, :], raw[:, c],
                                        slots[slot][0][:, 2 * c:2 * c + 2, :].bitcast(F32),
                                        ALU.subtract).then_inc(lo_split, 1)

            def variance(norm, t):
                dve.wait_ge(ss_ready, 4 * norm + t + 1)
                if norm == 4 and t == TT - 1:
                    nc.vector.tensor_tensor(ssum[:, t:t + 1], ssum[:, t:t + 1], ssum[:, 0:1],
                                            ALU.add).then_inc(sum_joined, 1)
                    dve.wait_ge(sum_joined, 1)
                nc.vector.tensor_scalar(var[:, t:t + 1], ssum[:, t:t + 1], 1.0 / D, EPS, ALU.mult,
                                        ALU.add).then_inc(var_ready, 1)

            def normed(norm, t):
                if t == 0:
                    dve.wait_ge(gain_landed, 16 * (norm + 1))
                dve.wait_ge(rstd_ready, 4 * norm + t + 1)
                if norm < 4 and t >= 2:
                    dve.wait_ge(xnT_done, 8 * norm + 2 * (t - 2) + 2)
                if norm == 4 and t >= 2:
                    dve.wait_ge(out_saved[t % 2], 16)
                halves = 2 if norm == 4 and t == TT - 1 else 1
                for f in range(halves):
                    c = slice(f * D // halves, (f + 1) * D // halves)
                    nc.vector.scalar_tensor_tensor(out=xn[:, t % 2, c], in0=x[:, t, c], scalar=rstd[:, t:t + 1],
                                                   in1=gain[:, c], op0=ALU.mult, op1=ALU.mult).then_inc(xn_ready, 1)

            def hT_parts(norm, t):
                for b in range(2):
                    dve.wait_ge(hT_hi, 8 * norm + 2 * t + b + 1)
                    hi = hT[0][:, 4 * b:4 * b + 4, P * t:P * t + P].bitcast(F32)
                    nc.vector.tensor_tensor(hT[1][:, 4 * b:4 * b + 4, P * t:P * t + P],
                                            bank[4 + 2 * (t % 2) + b][:, :].rearrange("p (k n) -> p k n", k=4),
                                            hi, ALU.subtract).then_inc(hT_lo, 1)

            def residual(parity, f, t, jobs_done):
                dve.wait_ge(job_done, jobs_done)
                v = x[:, t, 512 * f:512 * f + 512]
                nc.vector.tensor_tensor(v, bank[parity][:, :], v, ALU.add).then_inc(dev, 1)

            def norm_of(t):
                variance(0, t)
                normed(0, t)

            norm_of(0)
            split(0, 0, 0)
            hT_parts(0, 0)
            split(0, 1, 0)
            norm_of(1)
            split(0, 2, 0)
            hT_parts(0, 1)
            split(0, 3, 0)
            norm_of(2)
            norm_of(3)
            hT_parts(0, 2)
            hT_parts(0, 3)
            dve.wait_ge(ident_landed, 16)
            dve.wait_ge(const_landed, 16 * 4)
            nc.vector.tensor_copy(ident_bf[:, :], ident[:, :]).then_inc(consts_made, 1)
            nc.vector.tensor_copy(causal_bf[:, :], causal).then_inc(consts_made, 1)
            dve.wait_ge(wf_hi, 1)
            nc.vector.tensor_tensor(wf_stack[:, :, 32:GATE_COLS], wf, wf_stack[:, :, 0:NFOX].bitcast(F32),
                                    ALU.subtract).then_inc(wf_lo, 1)

            def logits(h, u):
                if h == 0 and u == 0:
                    dve.wait_ge(negc_ready, 1)
                if u == 0:
                    if h < 8:
                        dve.wait_ge(table_ready, h + 1)
                    else:
                        dve.wait_ge(bias_landed[h % 2], 16 * ((h - 8) // 2 + 1))
                if h >= 2 and u == 0:
                    dve.wait_ge(pv_done, h - 1)
                dve.wait_ge(score_done, 3 * h + u + 1)
                col = 0
                for tb in UNITS[u]:
                    n = P * (tb + 1)
                    c = ORDER.index(tb)
                    tab = table[:, h % 2, S - n:S] if h < 8 else table[:, h % 2, 0:n]
                    nc.vector.tensor_tensor_reduce(
                        out=prob[:, h % 2, OFF[tb]:OFF[tb] + n], in0=bank[2 + (3 * h + u) % 2][:, col:col + n],
                        in1=tab, scale=-1.0, scalar=BIG, op0=ALU.add, op1=ALU.min,
                        accum_out=negmax[:, h % 2, c:c + 1]).then_inc(logit_ready, 1)
                    col += n

            def copy_turned(g, u):
                dve.wait_ge(ptT_done, 3 * g + u + 1)
                o, n = OFF[UNITS[u][0]], (512, 384, 384)[u]
                nc.vector.tensor_copy(probT[:, o:o + n], bank[4 + (3 * g + u) % 2][:, 0:n]).then_inc(pt_v, 1)

            def normalise(pair):
                dve.wait_ge(prob_ready, 8 * (pair + 1))
                if pair == 0:
                    dve.wait_ge(negc_saved, 16)
                if pair:
                    dve.wait_ge(oT_done, pair)
                    dve.wait_ge(o_norm, pair)
                nc.vector.reciprocal(rden[:, :], den[:, pair % 2, :]).then_inc(rden_ready, 1)
                dve.wait_ge(rden_ready, pair + 1)
                dve.wait_ge(pv_done, 2 * (pair + 1))
                nc.vector.tensor_tensor(o_sb.rearrange("p (k n) -> p k n", k=8),
                                        bank[6][:, :].rearrange("p (k n) -> p k n", k=8),
                                        rden[:, :].rearrange("p (k o) -> p k o", o=1).to_broadcast([P, 8, HD]),
                                        ALU.mult).then_inc(o_norm, 1)

            def output_lo(pair):
                dve.wait_ge(oT_hi, pair + 1)
                nc.vector.tensor_tensor(oT[1][:, pair, :], bank[7][:, :], oT[0][:, pair, :].bitcast(F32),
                                        ALU.subtract).then_inc(oT_lo, 1)

            def step(h, g, v, pair):
                for u in range(3):
                    if h is not None:
                        logits(h, u)
                    if g is not None and not PT_BY_SCALAR[u]:
                        copy_turned(g, u)
                if v is not None and v % 2 == 1:
                    normalise(v // 2)
                if pair is not None:
                    output_lo(pair)

            for n, (kind, i) in enumerate(E_PANELS):
                for q in range(4):
                    j = e_first_job(n) + q
                    if kind != "out":
                        split(n + 1, q, (n + 1) % 2)
                    if kind == "qk":
                        pair, which = 2 * i + q // 2, q % 2
                        dve.wait_ge(aev, e_aev(j))
                        st, src = pair % 2, bank[j % 2]
                        for head, own in enumerate(ROWS):
                            if which == 0:
                                last = nc.vector.scalar_tensor_tensor(
                                    out=q_stack[ROWS[1 - head], st, head, :], in0=src[own, :], scalar=HD ** -0.5,
                                    in1=q_stack[own, st, head, :].bitcast(F32), op0=ALU.mult, op1=ALU.subtract)
                            else:
                                last = nc.vector.tensor_tensor(k_lo[own, st, :], src[own, :],
                                                               k_stack[own, st, head, :].bitcast(F32), ALU.subtract)
                        last.then_inc(lev, 1)
                    if kind == "out":
                        if i == 0 and q < 3:
                            dve.wait_ge(x_landed[q], 32)
                        residual(out_bank(j), i, q, j + 1)
                        split(n + 1, q, (n + 1) % 2)
                    if kind == "out" and i == 1:
                        variance(1, q)
                        normed(1, q)
                        if q >= 1:
                            hT_parts(1, q - 1)
                    for st in STEPS.get(j, []):
                        step(*st)
                if n == 5:
                    for st in TAIL:
                        step(*st)
                if n == 0:
                    dve.wait_ge(gate_low, 1)
                    nc.vector.scalar_tensor_tensor(out=gate[:, 0, :], in0=bank[GATE_JOB % 2][0:NFOX, :],
                                                   scalar=bias_f[:, 0:1], in1=gate[:, 2, :], op0=ALU.add,
                                                   op1=ALU.add).then_inc(dev, 1)
                    dve.wait_ge(dev, 1)
                    nc.vector.scalar_tensor_tensor(out=gate[:, 1, :], in0=gate[:, 0, :], scalar=-1.0, in1=gate[:, 0, :],
                                                   op0=ALU.mult, op1=ALU.max).then_inc(gate_abs, 1)
                    nc.vector.tensor_scalar(gate[:, 3, :], gate[:, 0, :], 0.0, None, ALU.min).then_inc(gate_min, 1)
                    dve.wait_ge(gate_min, 1)
                    dve.wait_ge(gate_ln, 1)
                    nc.vector.tensor_tensor_scan(negc, gate[:, 1, :], gate[:, 3, :], 0.0, ALU.add,
                                                 ALU.subtract).then_inc(negc_ready, 1)
            hT_parts(1, TT - 1)

            def mlp(c, pan, jobs, avs, hids, norm=None):
                for j in range(8):
                    split(pan + 4 * c + j // 4 + 1, j % 4, (j // 4 + 1) % 2)
                    dve.wait_ge(hid_lo, hids + 8 * c + j - 1) if (hids or j >= 2 or not isinstance(c, int)) else None
                    dve.wait_ge(aev, avs + 8 * c + j + 1)
                    nc.vector.tensor_tensor(sq_sb[:, j % 2, :], relu_sb[:, j % 2, :], relu_sb[:, j % 2, :],
                                            ALU.mult).then_inc(sq_ready, 1)
                    dve.wait_ge(hid_hi, hids + 8 * c + j + 1)
                    nc.vector.tensor_tensor(hid[1][:, j, :], sq_sb[:, j % 2, :], hid[0][:, j, :].bitcast(F32),
                                            ALU.subtract).then_inc(hid_lo, 1)
                for q in range(8):
                    if not (norm == 4 and q >= 4):
                        split(pan + 4 * c + 3 + q // 4, q % 4, (q // 4 + 1) % 2)
                    residual((jobs + q) % 2, q // 4, q % 4, jobs + 16 * c + 8 + q + 1)
                    if norm is not None and q >= 4:
                        t = q % 4
                        variance(norm, t)
                        normed(norm, t)
                        if t >= 1 and norm < 4:
                            hT_parts(norm, t - 1)
                if norm is not None and norm < 4:
                    hT_parts(norm, TT - 1)

            mlp(0, PAN_M0, JOB_M0, AEV_M0, 0)
            with dve.Fori(1, CHUNKS - 1) as c:
                mlp(c, PAN_M0, JOB_M0, AEV_M0, 0)
            mlp(CHUNKS - 1, PAN_M0, JOB_M0, AEV_M0, 0, norm=2)

            def r_split(n, s):
                for c in range(4):
                    split(n + 1, c, 1 - s)

            def r_lo(h, n, s, stage):
                for q in range(4):
                    split(n + 1, q, 1 - s)
                    src = bank[first_bank(JOB_O, q) if isinstance(h, int) and stage == "qk" else (JOB_O + q) % 2]
                    if stage == "qk":
                        hi, lo = (rq_parts[:, a, q // 2, q % 2, :] for a in range(2))
                    else:
                        hi, lo = (rv_parts[a][:, q, :] for a in range(2))
                    dve.wait_ge(aev, AEV_O + 12 * h + (0 if stage == "qk" else 4) + q + 1)
                    nc.vector.tensor_tensor(lo, src[:, :], hi.bitcast(F32), ALU.subtract).then_inc(lev, 1)

            def r_decay(h, table_row):
                def product(s):
                    n = S - P * s
                    if s == 0 and isinstance(h, int):
                        dve.wait_ge(xn_ready, 12)
                    if s >= 2:
                        dve.wait_ge(att_ready, 4 * h + s - 1)
                    dve.wait_ge(rs_done, 4 * h + s + 1)
                    nc.vector.tensor_tensor(att_tmp[:, s % 2, 0:n], bank[2 + s % 2][:, 0:n],
                                            table_row(n), ALU.mult).then_inc(att_prod, 1)

                def low(s):
                    o, n = ATT_OFF[s], S - P * s
                    dve.wait_ge(att_hi, 4 * h + s + 1)
                    nc.vector.tensor_tensor(att_parts[:, 1, o:o + n], att_tmp[:, s % 2, 0:n],
                                            att_parts[:, 0, o:o + n].bitcast(F32), ALU.subtract).then_inc(att_ready, 1)

                product(0)
                for s in range(1, 4):
                    product(s)
                    low(s - 1)
                low(3)

            def r_norm(h):
                def stats(t):
                    nc.vector.bn_stats(gn_stats[:, t, :], bank[4 + t][:, :]).then_inc(gn_st, 1)

                def aggregate(t):
                    nc.vector.bn_aggr(gn_mv[:, t, :], gn_stats[:, t, :]).then_inc(gn_ag, 1)

                dve.wait_ge(ro_done, 4 * h + 1)
                stats(0)
                dve.wait_ge(ro_done, 4 * h + 2)
                dve.wait_ge(gn_st, 4 * h + 1)
                stats(1)
                aggregate(0)
                for t in range(4):
                    dve.wait_ge(gn_ag, 4 * h + t + 1)
                    if t < 2:
                        dve.wait_ge(ro_done, 4 * h + t + 3)
                        dve.wait_ge(gn_st, 4 * h + t + 2)
                        stats(t + 2)
                    if t == 2:
                        dve.wait_ge(gn_st, 4 * h + 4)
                    nc.vector.tensor_scalar(gn_var[:, t:t + 1], gn_mv[:, t, 1:2], EPS, None, ALU.add).then_inc(gn_v, 1)
                    if t < 3:
                        aggregate(t + 1)
                    dve.wait_ge(aev, AEV_O + 12 * h + 8 + t + 1)
                    nc.vector.scalar_tensor_tensor(out=y_sb[:, t, :], in0=bank[4 + t][:, :], scalar=gn_mv[:, t, 0:1],
                                                   in1=y_sb[:, t, :], op0=ALU.subtract,
                                                   op1=ALU.mult).then_inc(y_part, 1)

            def r_turn(h):
                for k in range(4):
                    dve.wait_ge(yT_hi, 4 * h + k + 1)
                    nc.vector.tensor_tensor(yT[1][:, k, :], bank[4 + k][:, :], yT[0][:, k, :].bitcast(F32),
                                            ALU.subtract).then_inc(yT_lo, 1)

            def r_out(n, s, jobs, norm=None):
                for q in range(8):
                    f, t = out_order(norm, q)
                    residual((JOB_O + q) % 2, f, t, jobs + q + 1)
                    if q % 2 == 0:
                        split(n + 1, q // 2, 1 - s)
                    if norm is not None and f == 1:
                        variance(norm, t)
                        normed(norm, t)
                        if t >= 1:
                            hT_parts(norm, t - 1)
                if norm is not None:
                    hT_parts(norm, TT - 1)

            dve.wait_ge(decay_landed, 16)
            r_lo(0, PAN_O, 0, "qk")
            r_lo(0, PAN_O + 1, 1, "v")
            r_decay(0, lambda n: decay[:, 0, 0:n])
            r_split(PAN_O + 2, 0)
            r_norm(0)
            with dve.Fori(1, RH) as h:
                jb = JOB_O - 8 + 20 * h
                r_lo(h, PAN_O - 1 + 4 * h, 1, "qk")
                r_turn(h - 1)
                r_lo(h, PAN_O + 4 * h, 0, "v")
                r_decay(h, lambda n: decay[:, bass.ds(h, 1), 0:n].rearrange("p a n -> p (a n)"))
                r_split(PAN_O + 1 + 4 * h, 1)
                r_norm(h)
                r_out(PAN_O + 2 + 4 * h, 0, jb + 12)
            r_turn(RH - 1)
            r_out(PAN_O + 15, 1, JOB_O + 72, norm=3)

            with dve.Fori(0, CHUNKS - 1) as c:
                mlp(c, PAN_M1, JOB_M1, AEV_M1, 32)
            mlp(CHUNKS - 1, PAN_M1, JOB_M1, AEV_M1, 32, norm=4)

        @block.gpsimd
        def _(pool):
            nc.gpsimd.memset(arena[:, 10496:10752], 0.0).then_inc(zeros_made, 1)
            nc.gpsimd.memset(half_neg[:, :], -0.5).then_inc(half_made, 1)

            def load_gain(norm):
                if norm:
                    pool.wait_ge(xn_ready, 4 * norm)
                pool.dma_start(gain[:, :], gains[norm].to_broadcast([P, D])).then_inc(gain_landed, 16)

            def inv_std(norm):
                for t in range(TT):
                    pool.wait_ge(var_ready, 4 * norm + t + 1)
                    nc.gpsimd.tensor_tensor(rstd[:, t:t + 1], var[:, t:t + 1], half_neg[:, :],
                                            ALU.pow).then_inc(rstd_ready, 1)

            load_gain(0)
            pool.wait_ge(half_made, 1)
            inv_std(0)
            load_gain(1)

            for h in range(8):
                if h == 0:
                    pool.wait_ge(consts_made, 2)
                if h >= 2:
                    pool.wait_ge(logit_ready, 4 * (h - 1))
                nc.gpsimd.tensor_scalar(table[:, h % 2, :], delta, -(2.0 ** -(h + 1)), None,
                                        ALU.mult).then_inc(table_tmp, 1)
                pool.wait_ge(table_tmp, h + 1)
                nc.gpsimd.tensor_tensor(table[:, h % 2, :], table[:, h % 2, :], lncount,
                                        ALU.add).then_inc(table_ready, 1)
                if h == 1:
                    pool.wait_ge(negc_ready, 1)
                    pool.dma_start(negc_dram, negc).then_inc(negc_saved, 16)
            pool.wait_ge(negc_saved, 16)
            for h in range(8, 16):
                pool.wait_ge(logit_ready, 4 * (h - 1))
                pool.dma_start(table[:, h % 2, :], negc_dram[h - 8:h - 7, :].to_broadcast([P, S])
                               ).then_inc(bias_landed[h % 2], 16)
            inv_std(1)
            load_gain(2)
            pool.dma_start(decay, c_decay).then_inc(decay_landed, 16)
            inv_std(2)

            def gn_inv_std(h):
                for t in range(4):
                    pool.wait_ge(gn_v, 4 * h + t + 1)
                    nc.gpsimd.tensor_tensor(gn_rstd[:, t:t + 1], gn_var[:, t:t + 1], half_neg[:, :],
                                            ALU.pow).then_inc(gn_r, 1)

            with pool.Fori(0, RH) as h:
                gn_inv_std(h)
            pool.wait_ge(att_ready, 4 * RH)
            load_gain(3)
            inv_std(3)
            load_gain(4)
            inv_std(4)


_INS = ["x", "norm_mix_g", "norm_ffn_g", "even_w_in", "even_b_f", "even_w_out", "odd_w_in", "odd_w_out",
        "ffn_w_in", "ffn_w_out", "final_g"]


def constants():
    p = np.arange(P)[:, None]
    j = np.arange(S)[None, :]
    eye = np.eye(P, dtype=np.float32)
    causal = np.where(np.arange(P)[None, :] > p, NEG, 0.0).astype(np.float32)
    dist = p + (S - P) - j
    count = (dist >= 0) * ((dist <= 128) * 1 + (dist % 4 == 0) + (dist % 16 == 0))
    lncount = np.where(count > 0, np.log(np.maximum(count, 1)), NEG).astype(np.float32)
    gamma = 1.0 - 2.0 ** (-5.0 - np.arange(RH, dtype=np.float32))
    log_g = np.log(gamma.astype(np.float32)).astype(np.float64)
    rel = j - p
    decay = np.where(rel[:, None, :] >= 0, np.exp(log_g[None, :, None] * np.maximum(rel, 0)[:, None, :]), 0.0) / 16.0
    return {"c_ident": eye, "c_causal": causal, "c_delta": np.maximum(dist, 0).astype(np.float32),
            "c_lncount": lncount, "c_decay": decay.astype(np.float32)}


def kernel(**inputs):
    import concourse.bacc as _bacc
    from concourse.bass_utils import run_bass_kernel_spmd as _run

    nc = _bacc.Bacc("TRN2", target_bir_lowering=False, num_devices=1)
    arrays, args = {}, []
    for name, a in [(n, inputs[n]) for n in _INS] + list(constants().items()):
        a = np.ascontiguousarray(a)
        arrays[f"in_{name}"] = a
        args.append(nc.dram_tensor(f"in_{name}", a.shape, mybir.dt.from_np(a.dtype), kind="ExternalInput").ap())
    args.append(nc.dram_tensor("out_0", (1, S, D), F32, kind="ExternalOutput").ap())
    negc_dram = nc.dram_tensor("negc_dram", (NFOX, S), F32, kind="Internal").ap()
    trunk(nc, *args, negc_dram)
    r = _run(nc, [arrays], core_ids=[0])
    return r.results[0]["out_0"]
```
